# Optimizing a Trainium2 kernel written in Bass

```python
import math
import jax, jax.numpy as jnp
from jax import lax
import numpy as np

D_MODEL = 2048
BATCH = 1
SEQ = 256
DEPTH = 2

D_MIX = D_MODEL
RET_HEADS = 4
RET_DIM = D_MIX // 4
RET_HEAD_DIM = RET_DIM // RET_HEADS
RET_CHUNK = 128
ROPE_BASE = 10000.0
HG_HEADS = 4
HG_DIM = D_MIX // 4
HG_HEAD_DIM = HG_DIM // HG_HEADS
HG_CHUNK = 64
M_DIM = D_MIX - RET_DIM - HG_DIM
M_HEAD_DIM = 64
M_HEADS = M_DIM // M_HEAD_DIM
M_GROUPS = 2
M_STATE = 128
M_CONV = 4
M_CHUNK = 128
M_CONV_DIM = M_DIM + 2 * M_GROUPS * M_STATE
D_FF = 4 * D_MODEL
DEEPNORM_ALPHA = (2 * DEPTH) ** 0.25
DEEPNORM_BETA = (8 * DEPTH) ** -0.25
LN_EPS = 1e-5
RMS_EPS = 1e-6
N_ADA = 6
IN_SPLITS = (RET_DIM, RET_DIM, RET_DIM, RET_DIM,
             HG_DIM, HG_DIM, HG_DIM, HG_DIM,
             M_DIM, M_CONV_DIM, M_HEADS)
IN_COLS = 4 * RET_DIM + 4 * HG_DIM + M_DIM + M_CONV_DIM + M_HEADS

kernel_name = "hymba_style_ret_hgrn2_ssd_deepnorm_adaln"

def layer_norm(x, g, b):
    xf = x.astype(jnp.float32)
    mu = jnp.mean(xf, axis=-1, keepdims=True)
    var = jnp.mean(jnp.square(xf - mu), axis=-1, keepdims=True)
    return ((xf - mu) * lax.rsqrt(var + LN_EPS) * g + b).astype(x.dtype)

def rms_norm(x):
    xf = x.astype(jnp.float32)
    return xf * lax.rsqrt(jnp.mean(jnp.square(xf), axis=-1, keepdims=True) + RMS_EPS)

def rotary(positions):
    inv_freq = 1.0 / (ROPE_BASE ** jnp.linspace(0.0, 1.0, RET_HEAD_DIM // 2, dtype=jnp.float32))
    ang = positions[..., None].astype(jnp.float32) * inv_freq
    return jnp.cos(ang)[:, :, None, :], jnp.sin(ang)[:, :, None, :]

def apply_rotary(t, cos, sin):
    half = t.shape[-1] // 2
    t1, t2 = t[..., :half], t[..., half:]
    return jnp.concatenate([t1 * cos - t2 * sin, t1 * sin + t2 * cos], axis=-1)

def chunked_scalar_decay(q, k, v, log_a, chunk):
    b, l, h, n = q.shape
    p = v.shape[-1]
    nc = l // chunk
    q = q.reshape(b, nc, chunk, h, n)
    k = k.reshape(b, nc, chunk, h, n)
    v = v.reshape(b, nc, chunk, h, p)
    cum = jnp.cumsum(log_a.astype(jnp.float32).reshape(b, nc, chunk, h), axis=2)
    mask = jnp.tril(jnp.ones((chunk, chunk), bool))[None, None, :, :, None]
    seg = cum[:, :, :, None, :] - cum[:, :, None, :, :]
    decay = jnp.exp(jnp.where(mask, seg, -jnp.inf))
    scores = jnp.einsum('bcihn,bcjhn->bcijh', q, k) * decay
    y_intra = jnp.einsum('bcijh,bcjhp->bcihp', scores, v)
    k_end = k * jnp.exp(cum[:, :, -1:, :] - cum)[..., None]
    states = jnp.einsum('bcjhn,bcjhp->bchnp', k_end, v)
    chunk_decay = jnp.exp(cum[:, :, -1, :])

    def step(s, inp):
        st, dc = inp
        return dc[..., None, None] * s + st, s

    s0 = jnp.zeros((b, h, n, p), jnp.float32)
    _, s_prev = lax.scan(step, s0, (jnp.moveaxis(states, 1, 0), jnp.moveaxis(chunk_decay, 1, 0)))
    s_prev = jnp.moveaxis(s_prev, 0, 1)
    y_inter = jnp.einsum('bcihn,bchnp->bcihp', q * jnp.exp(cum)[..., None], s_prev)
    return (y_intra + y_inter).reshape(b, l, h, p)

def chunked_vector_decay(q, k, v, log_f, chunk):
    b, l, h, dk = q.shape
    dv = v.shape[-1]
    nc = l // chunk

    def to_chunks(t):
        return jnp.moveaxis(t.reshape(b, nc, chunk, *t.shape[2:]), 1, 0)

    mask = jnp.tril(jnp.ones((chunk, chunk), bool))[None, :, :, None, None]

    def step(state, inp):
        qc, kc, vc, gc = inp
        cum = jnp.cumsum(gc, axis=1)
        rel = jnp.exp(jnp.where(mask, cum[:, :, None] - cum[:, None], -jnp.inf))
        scores = jnp.einsum('bihd,bjhd,bijhd->bijh', qc, kc, rel)
        y = (jnp.einsum('bijh,bjhv->bihv', scores, vc)
             + jnp.einsum('bihd,bhdv->bihv', qc * jnp.exp(cum), state))
        total = cum[:, -1]
        state = (jnp.exp(total)[..., None] * state
                 + jnp.einsum('bjhd,bjhv->bhdv', kc * jnp.exp(total[:, None] - cum), vc))
        return state, y

    s0 = jnp.zeros((b, h, dk, dv), jnp.float32)
    _, y = lax.scan(step, s0, (to_chunks(q), to_chunks(k), to_chunks(v),
                               to_chunks(log_f.astype(jnp.float32))))
    return jnp.moveaxis(y, 0, 1).reshape(b, l, h, dv)

def retention(q, k, v, g, positions):
    b, l, _ = q.shape
    q = q.reshape(b, l, RET_HEADS, RET_HEAD_DIM)
    k = k.reshape(b, l, RET_HEADS, RET_HEAD_DIM)
    v = v.reshape(b, l, RET_HEADS, RET_HEAD_DIM)
    cos, sin = rotary(positions)
    q = apply_rotary(q, cos, sin)
    k = apply_rotary(k, cos, sin) * (RET_HEAD_DIM ** -0.5)
    log_gamma = jnp.log(1.0 - jnp.exp2(-5.0 - jnp.arange(RET_HEADS, dtype=jnp.float32)))
    log_a = jnp.broadcast_to(log_gamma, (b, l, RET_HEADS))
    o = rms_norm(chunked_scalar_decay(q, k, v, log_a, RET_CHUNK))
    return jax.nn.silu(g.astype(jnp.float32)) * o.reshape(b, l, RET_DIM)

def hgrn2(q, f_raw, i, g, lb, norm_w):
    b, l, _ = q.shape
    f = lb + (1.0 - lb) * jax.nn.sigmoid(f_raw.astype(jnp.float32))
    log_f = jnp.log(f)
    k = 1.0 - f
    shp = (b, l, HG_HEADS, HG_HEAD_DIM)
    o = chunked_vector_decay(q.reshape(shp), k.reshape(shp), i.reshape(shp), log_f.reshape(shp), HG_CHUNK)
    o = rms_norm(o).reshape(b, l, HG_DIM) * norm_w
    return o * jax.nn.silu(g.astype(jnp.float32))

def causal_conv(u, w, bias):
    out = lax.conv_general_dilated(u, w.astype(u.dtype)[:, None, :], window_strides=(1,),
                                   padding=[(M_CONV - 1, 0)],
                                   dimension_numbers=('NWC', 'WIO', 'NWC'),
                                   feature_group_count=u.shape[-1])
    return out + bias

def mamba2(z, xbc, dt_raw, conv_w, conv_b, dt_bias, a_log, d_skip, norm_w):
    b, l, _ = z.shape
    xbc = jax.nn.silu(causal_conv(xbc, conv_w, conv_b))
    xs, bm, cm = jnp.split(xbc, [M_DIM, M_DIM + M_GROUPS * M_STATE], axis=-1)
    xs = xs.reshape(b, l, M_HEADS, M_HEAD_DIM)
    rep = M_HEADS // M_GROUPS
    bm = jnp.repeat(bm.reshape(b, l, M_GROUPS, M_STATE), rep, axis=2)
    cm = jnp.repeat(cm.reshape(b, l, M_GROUPS, M_STATE), rep, axis=2)
    dt = jax.nn.softplus(dt_raw.astype(jnp.float32) + dt_bias)
    a = -jnp.exp(a_log.astype(jnp.float32))
    y = chunked_scalar_decay(cm, bm, xs * dt[..., None], dt * a, M_CHUNK)
    y = y + xs * d_skip[:, None]
    y = y.reshape(b, l, M_DIM) * jax.nn.silu(z.astype(jnp.float32))
    y = rms_norm(y.reshape(b, l, M_GROUPS, M_DIM // M_GROUPS)).reshape(b, l, M_DIM)
    return y * norm_w

def hybrid_mixer(h, positions, lb, w_in, w_out, hg_norm_w, conv_w, conv_b, dt_bias, a_log, d_skip, m_norm_w):
    proj = h @ w_in
    idx = [int(s) for s in np.cumsum(IN_SPLITS)[:-1]]
    rq, rk, rv, rg, hq, hf, hi, hg, mz, mxbc, mdt = jnp.split(proj, idx, axis=-1)
    o_ret = retention(rq, rk, rv, rg, positions)
    o_hg = hgrn2(hq, hf, hi, hg, lb, hg_norm_w)
    o_m = mamba2(mz, mxbc, mdt, conv_w, conv_b, dt_bias, a_log, d_skip, m_norm_w)
    o = jnp.concatenate([o_ret, o_hg, o_m], axis=-1).astype(h.dtype)
    return o @ w_out

def setup_inputs(seed: int = 0) -> dict:
    key = jax.random.key(seed)
    ks = jax.random.split(key, 20)
    f32 = jnp.float32
    nrm = lambda k, shp, s: jax.random.normal(k, shp, f32) * s
    dt0 = jnp.exp(jax.random.uniform(ks[12], (DEPTH, M_HEADS), f32, math.log(1e-3), math.log(1e-1)))
    return {
        "x": nrm(ks[0], (BATCH, SEQ, D_MODEL), 1.0),
        "c": nrm(ks[1], (BATCH, D_MODEL), 1.0),
        "positions": jnp.tile(jnp.arange(SEQ, dtype=jnp.int32)[None], (BATCH, 1)),
        "lb_logits": nrm(ks[2], (DEPTH, HG_DIM), 0.1),
        "w_in": nrm(ks[3], (DEPTH, D_MODEL, IN_COLS), D_MODEL ** -0.5),
        "w_out": nrm(ks[4], (DEPTH, D_MIX, D_MODEL), D_MIX ** -0.5 * DEEPNORM_BETA),
        "w_ada": nrm(ks[5], (DEPTH, D_MODEL, N_ADA * D_MODEL), 0.3 * D_MODEL ** -0.5),
        "b_ada": nrm(ks[6], (DEPTH, N_ADA * D_MODEL), 0.02),
        "ln_g": 1.0 + nrm(ks[7], (DEPTH, 2, D_MODEL), 0.02),
        "ln_b": nrm(ks[8], (DEPTH, 2, D_MODEL), 0.02),
        "hg_norm_w": 1.0 + nrm(ks[9], (DEPTH, HG_DIM), 0.02),
        "m_conv_w": nrm(ks[10], (DEPTH, M_CONV, M_CONV_DIM), M_CONV ** -0.5),
        "m_conv_b": nrm(ks[11], (DEPTH, M_CONV_DIM), 0.02),
        "m_dt_bias": dt0 + jnp.log(-jnp.expm1(-dt0)),
        "m_a_log": jnp.log(jax.random.uniform(ks[13], (DEPTH, M_HEADS), f32, 1.0, 16.0)),
        "m_d": 1.0 + nrm(ks[14], (DEPTH, M_HEADS), 0.02),
        "m_norm_w": 1.0 + nrm(ks[15], (DEPTH, M_DIM), 0.02),
        "w1": nrm(ks[16], (DEPTH, D_MODEL, D_FF), D_MODEL ** -0.5),
        "w2": nrm(ks[17], (DEPTH, D_FF, D_MODEL), D_FF ** -0.5 * DEEPNORM_BETA),
    }

def reference(x, c, positions, lb_logits, w_in, w_out, w_ada, b_ada, ln_g, ln_b, hg_norm_w,
              m_conv_w, m_conv_b, m_dt_bias, m_a_log, m_d, m_norm_w, w1, w2):
    p = jax.nn.softmax(lb_logits.astype(jnp.float32), axis=0)
    lbs = jnp.cumsum(p, axis=0) - p[0]
    cond = jax.nn.silu(c)
    for l in range(DEPTH):
        ada = (cond @ w_ada[l] + b_ada[l])[:, None, :]
        sh_m, sc_m, g_m, sh_f, sc_f, g_f = jnp.split(ada, N_ADA, axis=-1)
        h = x * (1.0 + sc_m) + sh_m
        y = hybrid_mixer(h, positions, lbs[l], w_in[l], w_out[l], hg_norm_w[l], m_conv_w[l],
                         m_conv_b[l], m_dt_bias[l], m_a_log[l], m_d[l], m_norm_w[l])
        x = layer_norm(DEEPNORM_ALPHA * x + (1.0 + g_m) * y, ln_g[l, 0], ln_b[l, 0])
        h = x * (1.0 + sc_f) + sh_f
        y = jnp.square(jax.nn.relu(h @ w1[l])) @ w2[l]
        x = layer_norm(DEEPNORM_ALPHA * x + (1.0 + g_f) * y, ln_g[l, 1], ln_b[l, 1])
    return x


_drawn_inputs = setup_inputs


def setup_inputs(seed=0):
    import zlib

    import numpy as np

    out = dict(_drawn_inputs(seed))
    spreads = {}
    factors = {'lb_logits': 5.962, 'hg_norm_w': 8.0, 'm_conv_b': 5.687, 'm_d': 8.0, 'm_norm_w': 7.327}
    for name, (base, spread) in spreads.items():
        noise = np.random.default_rng([zlib.crc32(name.encode()), seed]).standard_normal(out[name].shape)
        drawn = base * np.exp(spread * noise) if base else spread * noise
        out[name] = __import__('jax').numpy.asarray(drawn.astype(out[name].dtype))
    for name, factor in factors.items():
        out[name] = (out[name] * factor).astype(out[name].dtype)
    return out
```

```python
import math
from contextlib import ExitStack

import numpy as np

import concourse.bass as bass
from concourse import mybir

ALU = mybir.AluOpType
ACT = mybir.ActivationFunctionType
AX = mybir.AxisListType
F32 = mybir.dt.float32
F32R = mybir.dt.float32r
BF16 = mybir.dt.bfloat16
I32 = mybir.dt.int32
ds = bass.ds

P = 128
D = 2048
SEQ = 256
DEPTH = 2
KT = D // P
DFF = 4 * D
IN_COLS = 6672
UW = 1024
RAW_SLOTS, W_SLOTS = 8, 4
ADA_LAG = 4
NPASS = 25
NUNIT = NPASS * KT
FF0 = 9
GROUPS = 4
ALPHA = (2 * DEPTH) ** 0.25
LN_EPS, RMS_EPS = 1e-5, 1e-6
COL0 = [2048, 3072, 5120, 6144, 0, 1024, 4096]
OUT_ORDER = [4, 5, 6, 7, 0, 1, 2, 3] + list(range(8, 16))
TWO_PI = 2 * math.pi
C1 = 6.28125
C2 = 0.001934814453125
C3 = TWO_PI - C1 - C2
MAGIC = 1.5 * 2.0 ** 23

K_ID, K_ML, K_TRI, K_DG = 0, 128, 128 + 9 * 128, 128 + 9 * 128 + 384
K_KEEP = K_DG + 1024
K_LM, K_FREQ = K_KEEP, K_KEEP + 1024
K_ALL = K_FREQ + 64
T_C, T_HGW, T_CB, T_MNW, T_CW, T_LB = 192, 208, 216, 240, 256, 352

LINKS = {"act": 5, "dve": 60, "pool": 7}


def constants():
    t = np.arange(P)[:, None]
    r = np.arange(P)[None, :]
    k = np.zeros((P, K_ALL), np.float32)
    k[:, K_ID:K_ID + P] = np.eye(P)
    for lv in range(7):
        s = 64 >> lv
        mid = (r // (2 * s)) * 2 * s + s
        k[:, K_ML + lv * P:K_ML + lv * P + P] = np.where(r >= mid, (t >= mid) & (t <= r), (t > r) & (t < mid))
        same = (t // (2 * s)) == (r // (2 * s))
        k[:, K_LM + lv * P:K_LM + lv * P + P] = same & (t % (2 * s) < s) & (r % (2 * s) >= s)
    k[:, K_ML + 7 * P:K_ML + 8 * P] = t > r
    k[:, K_ML + 8 * P:K_ML + 9 * P] = t <= r
    k[:, K_LM + 7 * P:K_LM + 8 * P] = np.eye(P)
    k[:, K_TRI:K_TRI + P] = t <= r
    k[:, K_TRI + P:K_TRI + 2 * P] = 1.0
    k[:, K_TRI + 2 * P:K_TRI + 3 * P] = t <= r
    i = np.arange(SEQ)[None, :]
    for h in range(4):
        lg = float(np.float32(math.log(1.0 - 2.0 ** (-5 - h))))
        k[:, K_DG + h * SEQ:K_DG + (h + 1) * SEQ] = np.where(i >= t, np.exp(lg * np.maximum(i - t, 0)), 0.0) * P ** -0.5
    expo = np.linspace(0.0, 1.0, 64, dtype=np.float32)
    k[:, K_FREQ:K_FREQ + 64] = np.float32(1.0) / (np.float32(10000.0) ** expo)
    return k


def hybrid_trunk(nc, x, c, positions, lb_logits, w_in, w_out, w_ada, b_ada, ln_g, ln_b, hg_norm_w,
                 m_conv_w, m_conv_b, m_dt_bias, m_a_log, m_d, m_norm_w, w1, w2, consts, out):
    with ExitStack() as ctx:
        place = {"at": (nc.sbuf_base + 63) // 64 * 64}

        def sb(name, shape, dt=F32, at=None):
            size = int(np.prod(shape[1:])) * (2 if dt == BF16 else 4)
            if at is None:
                at = place["at"]
                place["at"] += (size + 31) // 32 * 32
            t = nc.alloc_sbuf_tensor_at(name, shape, dt, offset=at)
            return t

        base = place["at"]
        X = sb("X", [P, 2, D])
        HTh = sb("HTh", [P, KT, SEQ], F32R)
        HTl = sb("HTl", [P, KT, SEQ], F32R)
        t2h_at = place["at"]
        T2h = sb("T2h", [P, KT, SEQ], F32R)
        t2l_at = place["at"]
        T2l = sb("T2l", [P, KT, SEQ], F32R)
        RAW = sb("RAW", [P, RAW_SLOTS, UW])
        WH = sb("WH", [P, W_SLOTS, UW], F32R)
        WL = sb("WL", [P, W_SLOTS, UW], F32R)
        ADR = sb("ADR", [P, 2, UW])
        ACC = sb("ACC", [P, UW])
        K = sb("K", [P, K_KEEP])
        LM = sb("LM", [P, 8 * P], BF16)
        COS = sb("COS", [P, 2, 64])
        SIN = sb("SIN", [P, 2, 64])
        PT = sb("PT", [P, 360])
        ADA = sb("ADA", [P, DEPTH * 96])
        CT = sb("CT", [P, KT])
        LBT = sb("LBT", [P, DEPTH * 4])
        OML = sb("OML", [P, DEPTH * 4])
        MD = sb("MD", [P, DEPTH * 16])
        DTB = sb("DTB", [16, DEPTH])
        NA = sb("NA", [16, DEPTH])
        SC = sb("SC", [P, 2, KT])
        SH = sb("SH", [P, 2, KT])
        GC = sb("GC", [P, KT])
        cLB = sb("cLB", [P, 4])
        cOML = sb("cOML", [P, 4])
        cHGW = sb("cHGW", [P, 4])
        cCB = sb("cCB", [P, 12])
        cCW = sb("cCW", [P, 4, 12])
        cMNW = sb("cMNW", [P, 8])
        cMD = sb("cMD", [P, 16])
        cDTB = sb("cDTB", [16, 1])
        cNA = sb("cNA", [16, 1])
        BN = sb("BN", [P, 2, 4, 6])
        MV = sb("MV", [P, 2, 2])
        NMR = sb("NMR", [P, 2])
        RV = sb("RV", [P, 8])
        RR = sb("RR", [P, 8])
        RA = sb("RA", [P, 8])
        SSQ = sb("SSQ", [P, 8])
        DTR = sb("DTR", [P, 2, 16])
        DTC = sb("DTC", [P, 2, 2, 16])
        CROSSK = sb("CROSSK", [P, P])
        AL1 = sb("AL1", [P, 1])
        IDLE = sb("IDLE", [P, 4])
        SM = sb("SM", [P, P])
        SX = sb("SX", [P, P])

        w_at = place["at"]
        KB = 1024

        def W(name, kb, shape, dt=F32):
            return sb(name, shape, dt, at=w_at + kb * KB)

        XS = W("XS", 0, [P, 2, 1024])
        QT = W("QT", 8, [P, 4, SEQ])
        KTt = W("KTt", 12, [P, 4, SEQ])
        LF = W("LF", 16, [P, 2, 512])
        V = W("V", 20, [P, 2, 512])
        SG = W("SG", 24, [P, 2, 512])
        MS = W("MS", 28, [P, 8, P])
        place["at"] += 32 * KB
        assert place["at"] <= nc.sbuf_usable_end, (place["at"], nc.sbuf_usable_end)
        E = sb("E", [P, 8, P], at=t2h_at)
        EQ = sb("EQ", [P, 8, P], at=t2l_at)
        U = sb("U", [P, 8, SEQ], at=t2h_at + 8 * KB)
        CV = sb("CV", [P, 8, SEQ], at=t2l_at + 8 * KB)
        XD = sb("XD", [P, 2, 1024], at=t2h_at + 8 * KB)
        BU = sb("BU", [P, 4, SEQ], at=t2l_at + 8 * KB)
        BC = W("BC", 8, [P, 4, SEQ])
        CB2 = W("CB2", 12, [P, 4, SEQ])
        SB = W("SB", 12, [P, 2, 384])
        DTW = [sb(f"DTW{i}", [16, SEQ], at=w_at + (28 + i) * KB) for i in range(4)]
        CUM = sb("CUM", [16, SEQ], at=t2l_at + 14 * KB)
        DTT = sb("DTT", [16, SEQ], at=t2l_at + 15 * KB)
        MW = sb("MW", [P, 2, 2, 384], at=t2l_at + 8 * KB)
        QK = W("QK", 20, [P, 2, 1024])
        RA1 = W("RA1", 16, [P, 1024])
        RB1 = W("RB1", 28, [P, 1024])
        RVv = W("RVv", 8, [P, 2, 512])
        RSG = W("RSG", 12, [P, 2, 512])
        RQT = sb("RQT", [P, 4, SEQ], at=t2h_at + 8 * KB)
        RKT = sb("RKT", [P, 4, SEQ], at=t2h_at + 12 * KB)
        SR = sb("SR", [P, 4, 384], at=t2l_at + 8 * KB)
        RO = W("RO", 28, [P, 2, 512])
        ZS = W("ZS", 20, [P, 2, 1024])
        JUNK = W("JUNK", 16, [P, 8, P])
        TX = W("TX", 0, [P, 4, SEQ])
        TM = {1: W("TM1", 20, [P, 4, SEQ]), 2: W("TM2", 8, [P, 4, SEQ])}
        TM[3] = TM[2]
        HJ = W("HJ", 0, [P, P])
        GB = W("GB", 8, [P, D])
        LNG = W("LNG", 16, [P, D])
        LNB = W("LNB", 24, [P, D])
        R = W("R", 0, [P, 2, 512])
        SQ = W("SQ", 4, [P, 2, 512])
        ST = W("ST", 0, [P, 3, P])
        LMs = W("LMs", 8, [P, 1024])
        FREQ = W("FREQ", 12, [P, 64])
        POSI = sb("POSI", [P, 2], I32, at=w_at + 13 * KB)
        POSF = W("POSF", 14, [P, 2])
        ANG = W("ANG", 16, [P, 2, 64])
        RND = W("RND", 17, [P, 2, 64])
        S2 = W("S2", 18, [P, 2, 64])
        E16 = W("E16", 19, [P, KT])
        LX = W("LX", 20, [P, 8])
        LMX = W("LMX", 21, [P, 4])
        AL = W("AL", 22, [16, DEPTH])

        PB = [ctx.enter_context(nc.psum_tensor(f"PB{i}", [P, 512], F32)) for i in range(8)]

        class Signal:

            def __init__(self, name, per=0, first=0):
                self.sem = ctx.enter_context(nc.semaphore(name))
                self.per, self.first = per, first

            def at(self, layer, count):
                return self.first + layer * self.per + count

        raw_in = [Signal(f"raw_in{i}", 16 * NUNIT // RAW_SLOTS, 16 * 64 // RAW_SLOTS) for i in range(RAW_SLOTS)]
        hi_done = Signal("hi_done", NUNIT)
        lo_done = Signal("lo_done", NUNIT, RAW_SLOTS)
        unit_done = Signal("unit_done", NUNIT, W_SLOTS)
        set_free = Signal("set_free", 7)
        ada_in = [Signal(f"ada_in{i}", 16 * 96) for i in range(2)]
        ada_mac = Signal("ada_mac", 192, 64 + 2)
        ada_sum = Signal("ada_sum", 12, 4)
        ada_cols = Signal("ada_cols", 12, 4)
        x_ready = Signal("x_ready", 8, 4)
        xT = Signal("xT", 16)
        hT_hi = Signal("hT_hi", 32)
        hT_ready = Signal("hT_ready", 32)
        cols_set = Signal("cols_set", 2)
        t2_T = Signal("t2_T", 3)
        t2_hi = Signal("t2_hi", 16)
        t2_ready = Signal("t2_ready", 16)
        rs_in = Signal("rs_in", 5)
        rs_act = Signal("rs_act", 5)
        rs_out = Signal("rs_out", 5)
        hg_f = Signal("hg_f", 4)
        hg_k = Signal("hg_k", 1)
        hg_lnf = Signal("hg_lnf", 1)
        hg_logT = Signal("hg_logT", 1)
        hg_log = Signal("hg_log", 1)
        hg_x = Signal("hg_x", 8)
        hg_e = Signal("hg_e", 8)
        hg_eq = Signal("hg_eq", 8)
        hg_ek = Signal("hg_ek", 8)
        hg_s = Signal("hg_s", 8)
        hg_sm = Signal("hg_sm", 8)
        hg_sx = Signal("hg_sx", 4)
        hg_o = Signal("hg_o", 8)
        hg_oe = Signal("hg_oe", 8)
        hg_rows = Signal("hg_rows", 1)
        cv_in = Signal("cv_in", 12)
        cv_done = Signal("cv_done", 2)
        cv_act = Signal("cv_act", 2)
        dt_T = Signal("dt_T", 1)
        dt_abs = Signal("dt_abs", 1)
        dt_exp = Signal("dt_exp", 1)
        dt_u = Signal("dt_u", 1)
        dt_ln = Signal("dt_ln", 1)
        dt_cum = Signal("dt_cum", 1)
        dt_rows = Signal("dt_rows", 1)
        dt_ready = Signal("dt_ready", 1)
        xs_T = Signal("xs_T", 2)
        xs_rows = Signal("xs_rows", 2)
        xd_ready = Signal("xd_ready", 1)
        xsd_ready = Signal("xsd_ready", 1)
        m_s = Signal("m_s", 2)
        m_sm = Signal("m_sm", 2)
        m_cum = Signal("m_cum", 8)
        m_arg = Signal("m_arg", 8)
        m_exp = Signal("m_exp", 8)
        m_m = Signal("m_m", 8)
        m_y = Signal("m_y", 8)
        m_ye = Signal("m_ye", 2)
        m_z = Signal("m_z", 1)
        m_sq = Signal("m_sq", 1)
        m_rows = Signal("m_rows", 1)
        r_rot = Signal("r_rot", 1)
        r_T = Signal("r_T", 1)
        r_Te = Signal("r_Te", 1)
        r_s = Signal("r_s", 2)
        r_sm = Signal("r_sm", 4)
        r_o = Signal("r_o", 1)
        r_oe = Signal("r_oe", 1)
        r_rows = Signal("r_rows", 1)
        g_cols = Signal("g_cols", 3)
        g_bc = Signal("g_bc", 3)
        g_ready = Signal("g_ready", 3)
        gated = Signal("gated", 40)
        x_add = Signal("x_add", 40)
        ln_gb_in = Signal("ln_gb_in", 64)
        ln_norm = Signal("ln_norm", 8)
        ln_mul = Signal("ln_mul", 8)
        ff_relu = Signal("ff_relu", 32)
        ff_sq = Signal("ff_sq", 32)
        ff_hi = Signal("ff_hi", 32)
        ff_ready = Signal("ff_ready", 32)
        pro_st = Signal("pro_st")
        pro_in = Signal("pro_in")
        pro_x = Signal("pro_x")
        pro_T = Signal("pro_T")
        pro_pt = Signal("pro_pt")
        pro_act = Signal("pro_act")
        pro_dve = Signal("pro_dve")
        out_done = Signal("out_done")
        order = {e: Signal(f"{e}_order", LINKS[e]) for e in LINKS}

        class Order:

            def __init__(self, eng, sig):
                self.eng, self.sig, self.layer, self.n = eng, sig, None, 0

            def start(self, layer):
                if self.layer is None:
                    self.sig.first = self.n
                self.layer, self.n = layer, 0

            def __call__(self, ins):
                ins.then_inc(self.sig.sem, 1)
                self.n += 1
                self.eng.wait_ge(self.sig.sem, self.n if self.layer is None else self.sig.at(self.layer, self.n))

            def end(self, name):
                assert self.n == LINKS[name], (name, self.n)

        w_in_r = w_in.rearrange("l k n -> (l k) n")
        w_out_r = w_out.rearrange("l k n -> (l k) n")
        w_ada_r = w_ada.rearrange("l k n -> (l k) n")
        w1_r = w1.rearrange("l k n -> (l k) n")
        w2_r = w2.rearrange("l k n -> (l k) n")
        ln_g_r = ln_g.rearrange("l s n -> (l s) n")
        ln_b_r = ln_b.rearrange("l s n -> (l s) n")
        x_r = x.rearrange("b (r p) n -> p (b r) n", p=P)
        out_r = out.rearrange("b (r p) n -> p (b r) n", p=P)
        ident = K[:, K_ID:K_ID + P]
        ones = K[:, K_TRI + P:K_TRI + P + 1]

        HG_X, HG_X1, HG_S, HG_M = [3, 6, 9, 12], [4, 7, 10, 13], [5, 8, 11, 14], [6, 9, 12, 15]
        HG_O = [(2, 7), (2, 10), (2, 13), (3, 4), (3, 7), (3, 10), (3, 13), (4, 4)]
        M_CUM, M_ARG = [4, 5, 6, 7, 8, 9, 11, 12], [5, 6, 7, 8, 9, 10, 12, 13]
        M_MUL, M_Y = [6, 7, 8, 9, 10, 11, 13, 14], [7, 8, 9, 10, 12, 13, 14, 15]

        def ada_bank(p):
            return 1 if p < 4 else 3

        def width(p):
            return 528 if p == 3 else UW

        def bank(p, b):
            return PB[4 * (p % 2) + b]

        def work(p, b):
            return PB[4 * (1 - p % 2) + b]

        def ada_units(n, span, total):
            half, m = divmod(n, span)
            live = span - ADA_LAG
            if half >= total or m >= live:
                return []
            return [half * 16 + k for k in range(m * 16 // live, (m + 1) * 16 // live)]

        def ada_due(n, span, total):
            half, m = divmod(n, span)
            return half if half < total and m == span - 2 else None

        def bc(ap, shape):
            return ap.broadcast_to(shape)

        block = ctx.enter_context(nc.Block())

        @block.sync
        def _(sp):
            def ada_load(count, unit, row, col):
                sp.wait_ge(ada_mac.sem, count(unit + 1))
                sp.dma_start(ADR[:, unit % 2, :], w_ada_r[ds(row, P), ds(col, UW)]
                             ).then_inc(ada_in[unit % 2].sem, 16)

            def raw_load(layer, n, slot, src):
                sp.wait_ge(lo_done.sem, lo_done.at(layer, n + 1) - RAW_SLOTS)
                w = src.shape[1]
                sp.dma_start(RAW[:, slot, 0:w], src).then_inc(raw_in[slot].sem, 16)

            for a in range(64):
                if a >= RAW_SLOTS:
                    sp.wait_ge(ada_mac.sem, a - RAW_SLOTS + 3)
                sp.dma_start(RAW[:, a % RAW_SLOTS, :], w_ada_r[(a % 16) * P:(a % 16 + 1) * P,
                                                               (a // 16) * UW:(a // 16 + 1) * UW]
                             ).then_inc(raw_in[a % RAW_SLOTS].sem, 16)
            with sp.Fori(0, DEPTH) as layer:
                for p in range(FF0):
                    for kt in range(KT):
                        n = p * KT + kt
                        if p < 7:
                            src = w_in_r[ds(layer * D + kt * P, P), COL0[p]:COL0[p] + width(p)]
                        else:
                            src = w_out_r[ds(layer * D + OUT_ORDER[kt] * P, P), (p - 7) * UW:(p - 6) * UW]
                        raw_load(layer, n, n % RAW_SLOTS, src)
                        for a in ada_units(n - ADA_LAG, 24, 6) if n >= ADA_LAG else ():
                            ada_load(lambda k: ada_mac.at(layer, k) - 2, a, layer * D + (a % 16) * P,
                                     (4 + a // 16) * UW)
                with sp.Fori(0, GROUPS) as g:
                    def group(ada):
                        for m in range(4 * KT):
                            s, kt = divmod(m, KT)
                            if s < 2:
                                src = w1_r[ds(layer * D + kt * P, P), ds(g * D + s * UW, UW)]
                            else:
                                src = w2_r[ds(layer * DFF + g * D + kt * P, P), (s - 2) * UW:(s - 1) * UW]
                            raw_load(layer, FF0 * KT + g * 64 + m, m % RAW_SLOTS, src)
                            for a in ada_units(m - ADA_LAG, 32, 2) if ada and m >= ADA_LAG else ():
                                q = layer * 12 + 10 + g * 2 + a // 16
                                ada_load(lambda k: ada_mac.at(layer, 96 + g * 32 + k) - 2, a,
                                         ((q // 12) % 2) * D + (a % 16) * P, (q % 12) * UW)
                    with sp.If(g + 2 * layer < 3):
                        group(True)
                    with sp.Else():
                        group(False)
            for ch in range(4):
                sp.wait_ge(x_ready.sem, x_ready.at(DEPTH - 1, 4 + ch + 1))
                cols = slice(ch * 512, (ch + 1) * 512)
                sp.dma_start(out_r[:, :, cols], X[:, :, cols]).then_inc(out_done.sem, 16)
            sp.wait_ge(out_done.sem, 16 * 4)

        @block.gpsimd
        def _(pool):
            link = Order(pool, order["pool"])
            pool.memset(RV[:, :], 1.0)
            pool.memset(RR[:, :], 1.0).then_inc(unit_done.sem, W_SLOTS)
            pool.memset(AL1[:, :], ALPHA)
            pool.memset(IDLE[:, :], 0.0)
            pool.memset(SSQ[:, :], 1.0).then_inc(ada_mac.sem, 2)
            pool.dma_start(X[:, :, :], x_r).then_inc(pro_x.sem, 16)
            pool.wait_ge(pro_x.sem, 16)
            pool.memset(NMR[:, :], 0.0).then_inc(x_ready.sem, 4)

            def scale_x(layer, s):
                for ch in range(4):
                    pool.wait_ge(xT.sem, xT.at(layer, 8 * s + 2 * ch + 2))
                    xc = X[:, :, ch * 512:(ch + 1) * 512]
                    ins = pool.tensor_tensor(xc, xc, bc(AL1[:, :].unsqueeze(1), [P, 2, 512]), ALU.mult)
                link(ins)

            def add_y(layer, k, half):
                for b in range(4):
                    r, col = b // 2, half * UW + (b % 2) * 512
                    pool.wait_ge(gated.sem, gated.at(layer, k + b + 1))
                    xc = X[:, r, col:col + 512]
                    pool.tensor_tensor(xc, xc, R[:, b % 2, :], ALU.add).then_inc(x_add.sem, 1)

            def load_ln(layer, s):
                pool.dma_start(LNG[:, :], ln_g_r[ds(layer * 2 + s, 1), :].squeeze(0).partition_broadcast(P)
                               ).then_inc(ln_gb_in.sem, 16)
                pool.dma_start(LNB[:, :], ln_b_r[ds(layer * 2 + s, 1), :].squeeze(0).partition_broadcast(P)
                               ).then_inc(ln_gb_in.sem, 16)

            def ln_add(layer, s):
                for ch in range(4):
                    pool.wait_ge(ln_mul.sem, ln_mul.at(layer, 4 * s + ch + 1))
                    xc = X[:, :, ch * 512:(ch + 1) * 512]
                    pool.tensor_tensor(xc, xc, bc(LNB[:, ch * 512:(ch + 1) * 512].unsqueeze(1), [P, 2, 512]),
                                       ALU.add).then_inc(x_ready.sem, 1)

            with pool.Fori(0, DEPTH) as layer:
                link.start(layer)
                scale_x(layer, 0)
                for i in range(8):
                    h, t = divmod(i, 2)
                    kk = KTt[:, h, t * P:(t + 1) * P]
                    pool.wait_ge(hg_eq.sem, hg_eq.at(layer, i + 1))
                    if i == 0:
                        pool.wait_ge(hg_k.sem, hg_k.at(layer, 1))
                    if t == 0:
                        if h >= 1:
                            pool.wait_ge(hg_s.sem, hg_s.at(layer, i))
                        pool.tensor_tensor(CROSSK[:, :], E[:, 7, :], kk, ALU.mult)
                    pool.tensor_tensor(E[:, 0:7, :], E[:, 0:7, :], bc(kk.unsqueeze(1), [P, 7, P]), ALU.mult
                                       ).then_inc(hg_ek.sem, 1)
                pool.wait_ge(hg_oe.sem, hg_oe.at(layer, 8))
                link(pool.tensor_tensor(LF[:, :, :], LF[:, :, :], SG[:, :, :], ALU.mult))
                pool.wait_ge(rs_out.sem, rs_out.at(layer, 1))
                lf8 = LF[:, :, :].rearrange("p t (h d) -> p (t h) d", d=P)
                pool.tensor_tensor(lf8, lf8, bc(RR[:, 0:8].unsqueeze(2), [P, 8, P]), ALU.mult
                                   ).then_inc(hg_rows.sem, 1)
                pool.wait_ge(dt_ready.sem, dt_ready.at(layer, 1))
                pool.wait_ge(xs_rows.sem, xs_rows.at(layer, 2))
                for r in range(2):
                    xs = XS[:, r, :].rearrange("p (h d) -> p h d", d=64)
                    xd = XD[:, r, :].rearrange("p (h d) -> p h d", d=64)
                    ins = pool.tensor_tensor(xd, xs, bc(DTC[:, r, 0, :].unsqueeze(2), [P, 16, 64]), ALU.mult)
                ins.then_inc(xd_ready.sem, 1)
                for r in range(2):
                    xs = XS[:, r, :].rearrange("p (h d) -> p h d", d=64)
                    ins = pool.tensor_tensor(xs, xs, bc(cMD[:, :].unsqueeze(2), [P, 16, 64]), ALU.mult)
                ins.then_inc(xsd_ready.sem, 1)
                pool.wait_ge(set_free.sem, set_free.at(layer, 5))
                for r in range(2):
                    qk = QK[:, r, :].rearrange("p (h f) -> p h f", f=64)
                    a1 = RA1[:, :].rearrange("p (h f) -> p h f", f=64)
                    b1 = RB1[:, :].rearrange("p (h f) -> p h f", f=64)
                    pool.tensor_tensor(a1, qk, bc(COS[:, r, :].unsqueeze(1), [P, 16, 64]), ALU.mult)
                    link(pool.tensor_tensor(b1, qk, bc(SIN[:, r, :].unsqueeze(1), [P, 16, 64]), ALU.mult))
                    qh = QK[:, r, :].rearrange("p (h s f) -> p h s f", s=2, f=64)
                    ah = RA1[:, :].rearrange("p (h s f) -> p h s f", s=2, f=64)
                    bh = RB1[:, :].rearrange("p (h s f) -> p h s f", s=2, f=64)
                    pool.tensor_tensor(qh[:, :, 0, :], ah[:, :, 0, :], bh[:, :, 1, :], ALU.subtract)
                    ins = pool.tensor_tensor(qh[:, :, 1, :], bh[:, :, 0, :], ah[:, :, 1, :], ALU.add)
                    if r == 0:
                        link(ins)
                ins.then_inc(r_rot.sem, 1)
                pool.wait_ge(r_oe.sem, r_oe.at(layer, 1))
                link(pool.tensor_tensor(RO[:, :, :], RO[:, :, :], RSG[:, :, :], ALU.mult))
                pool.wait_ge(rs_out.sem, rs_out.at(layer, 2))
                ro8 = RO[:, :, :].rearrange("p t (h d) -> p (t h) d", d=P)
                pool.tensor_tensor(ro8, ro8, bc(RR[:, 0:8].unsqueeze(2), [P, 8, P]), ALU.mult
                                   ).then_inc(r_rows.sem, 1)
                pool.wait_ge(t2_T.sem, t2_T.at(layer, 3))
                load_ln(layer, 0)
                add_y(layer, 0, 0)
                add_y(layer, 4, 1)
                ln_add(layer, 0)
                pool.wait_ge(x_ready.sem, x_ready.at(layer, 4))
                load_ln(layer, 1)
                scale_x(layer, 1)
                pool.tensor_tensor(IDLE[:, 1:2], IDLE[:, 0:1], IDLE[:, 0:1], ALU.mult)
                with pool.Fori(0, GROUPS) as g:
                    with pool.If(g > 0):
                        add_y(layer, 4 + g * 8, 1)
                    for i in range(8):
                        pool.wait_ge(ff_relu.sem, ff_relu.at(layer, g * 8 + i + 1))
                        if i >= 2:
                            pool.wait_ge(ff_ready.sem, ff_ready.at(layer, g * 8 + i - 1))
                        pool.tensor_tensor(SQ[:, i % 2, :], R[:, i % 2, :], R[:, i % 2, :], ALU.mult
                                           ).then_inc(ff_sq.sem, 1)
                    add_y(layer, 8 + g * 8, 0)
                add_y(layer, 36, 1)
                ln_add(layer, 1)
                link.end("pool")

        @block.scalar
        def _(act):
            link = Order(act, order["act"])
            loads = [
                (K[:, P:], consts[:, P:K_KEEP]), (LMs[:, :], consts[:, K_LM:K_LM + 1024]),
                (FREQ[:, :], consts[:, K_FREQ:K_FREQ + 64]),
                (POSI[:, :], positions.rearrange("b (r p) -> p (b r)", p=P)),
                (DTB[:, :], m_dt_bias.rearrange("l h -> h l")), (AL[:, :], m_a_log.rearrange("l h -> h l")),
                (MD[:, :], m_d.rearrange("l h -> (l h)").partition_broadcast(P)),
            ]
            bt = b_ada.rearrange("l (t p) -> (l t) p", p=P)
            first = [(ST[:, 0, :], bt[0:128, :]), (ST[0:64, 1, :], bt[128:192, :]),
                      (ST[64:80, 1, :], c.rearrange("b (t p) -> (b t) p", p=P)),
                      (ST[80:88, 1, :], hg_norm_w.rearrange("l (t p) -> (l t) p", p=P)),
                      (ST[88:112, 1, :], m_conv_b.rearrange("l (t p) -> (l t) p", p=P)),
                      (ST[112:128, 1, :], m_norm_w.rearrange("l (t p) -> (l t) p", p=P)),
                      (ST[0:96, 2, :], m_conv_w.rearrange("l k (t p) -> (l k t) p", p=P)),
                      (ST[96:104, 2, :], lb_logits.rearrange("l (t p) -> (l t) p", p=P))]
            for dst, src in [(K[:, 0:P], consts[:, 0:P])] + first:
                act.dma_start(dst, src).then_inc(pro_st.sem, 16)
            for dst, src in loads:
                act.dma_start(dst, src, allow_slow_non_contiguous=True).then_inc(pro_in.sem, 16)
            act.wait_ge(pro_T.sem, 1)
            act.activation(PT[:, :], PB[0][:, 0:360], ACT.Copy).then_inc(pro_pt.sem, 1)
            act.wait_ge(pro_pt.sem, 1)
            act.activation(E16[:, :], PT[:, T_C:T_C + KT], ACT.Exp, scale=-1.0).then_inc(pro_act.sem, 1)
            act.wait_ge(pro_in.sem, 16 * 7)
            act.activation(AL[:, :], AL[:, :], ACT.Exp).then_inc(pro_act.sem, 1)
            act.wait_ge(pro_dve.sem, 1)
            act.activation(LX[:, :], LX[:, :], ACT.Exp).then_inc(pro_act.sem, 1)
            act.wait_ge(pro_dve.sem, 2)
            act.activation(SIN[:, :, :], ANG[:, :, :], ACT.Sin).then_inc(pro_act.sem, 1)
            act.activation(S2[:, :, :], ANG[:, :, :], ACT.Sin, scale=0.5).then_inc(pro_act.sem, 1)

            def hi_split(layer, n, m, loads_before, w=UW):
                act.wait_ge(raw_in[m % RAW_SLOTS].sem, raw_in[0].at(layer, (loads_before + 1) * 16))
                act.wait_ge(unit_done.sem, unit_done.at(layer, n + 1) - W_SLOTS)
                act.activation(WH[:, m % W_SLOTS, 0:w], RAW[:, m % RAW_SLOTS, 0:w], ACT.Copy
                               ).then_inc(hi_done.sem, 1)

            def t_out(tt_, src, k, dst, hi_sig, scale, bias):
                for j in range(2):
                    s = scale[:, j:j + 1] if scale is not None else 1.0
                    b = bias[:, j:j + 1] if bias is not None else 0.0
                    cols = src[:, j * SEQ:(j + 1) * SEQ]
                    act.activation(tt_[:, (k + j) % 4, :], cols, ACT.Identity, bias=b, scale=s)
                    act.activation(dst[:, j, :], cols, ACT.Identity, bias=b, scale=s).then_inc(hi_sig.sem, 1)

            def h_chunk(layer, s, ch):
                if ch == 0:
                    act.wait_ge(cols_set.sem, cols_set.at(layer, s + 1))
                for b in (2 * ch, 2 * ch + 1):
                    kt = 2 * b
                    if kt >= 4:
                        act.wait_ge(hT_ready.sem, hT_ready.at(layer, 16 * s + kt - 2))
                    act.wait_ge(xT.sem, xT.at(layer, 8 * s + b + 1))
                    t_out(TX, work(s * FF0, b % 4), kt, HTh[:, kt:kt + 2, :], hT_hi, SC[:, s, kt:kt + 2],
                          SH[:, s, kt:kt + 2])

            def t2_chunk(layer, which, p, banks, kt0, count0, weights=None):
                act.wait_ge(t2_T.sem, t2_T.at(layer, which))
                for i, b in enumerate(banks):
                    kt, k = kt0 + 2 * i, count0 + 2 * i
                    if k >= 6:
                        act.wait_ge(t2_ready.sem, t2_ready.at(layer, k - 2))
                    t_out(TM[which], work(p, b), k, T2h[:, kt:kt + 2, :], t2_hi,
                          None if weights is None else weights[:, 2 * i:2 * i + 2], None)

            def rsqrt(layer, k, cols):
                act.wait_ge(rs_in.sem, rs_in.at(layer, k))
                link(act.activation(RA[:, 0:cols], RV[:, 0:cols], ACT.Ln))
                act.activation(RR[:, 0:cols], RA[:, 0:cols], ACT.Exp, scale=-0.5).then_inc(rs_act.sem, 1)

            def layer_norm_rows(layer, s):
                rsqrt(layer, 4 + s, 2)
                act.wait_ge(rs_out.sem, rs_out.at(layer, 4 + s))
                for ch in range(4):
                    for r in range(2):
                        xc = X[:, r, ch * 512:(ch + 1) * 512]
                        ins = act.activation(xc, xc, ACT.Identity, bias=NMR[:, r:r + 1], scale=RR[:, r:r + 1])
                    ins.then_inc(ln_norm.sem, 1)

            def gate_rows(layer, k, p, parts):
                act.wait_ge(g_bc.sem, g_bc.at(layer, k))
                for i, b in enumerate(parts):
                    ins = act.activation(GB[:, b * 512:(b + 1) * 512], work(p, i)[:, :], ACT.Copy)
                ins.then_inc(g_ready.sem, 1)

            def evacuate(layer, p):
                act.wait_ge(unit_done.sem, unit_done.at(layer, KT * (p + 1)))
                halves = [(r, h) for r in range(2) for h in range(2)]
                if p == 0:
                    act.activation(QT[:, 0:2, :], bank(0, 0)[:, :], ACT.Copy)
                    act.activation(QT[:, 2:4, :], bank(0, 1)[:, :], ACT.Copy)
                    act.activation(EQ[:, 0:4, :], bank(0, 2)[:, :], ACT.Sigmoid)
                    ins = act.activation(EQ[:, 4:8, :], bank(0, 3)[:, :], ACT.Sigmoid)
                elif p in (1, 5):
                    val, gate = (V, SG) if p == 1 else (RVv, RSG)
                    for r in range(2):
                        act.activation(val[:, r, :], bank(p, 2 * r)[:, :], ACT.Copy)
                    for r in range(2):
                        ins = act.activation(gate[:, r, :], bank(p, 2 * r + 1)[:, :], ACT.Silu)
                elif p == 2:
                    for b in range(4):
                        ins = act.activation(U[:, 2 * b:2 * b + 2, :], bank(2, b)[:, :], ACT.Copy)
                elif p == 3:
                    act.activation(BU[:, 0:2, :], bank(3, 0)[:, :], ACT.Copy)
                    act.activation(BU[:, 2:4, :], bank(3, 1)[:, :], ACT.Copy)
                    act.activation(DTR[:, 0, :], bank(3, 2)[:, 0:16], ACT.Copy)
                    ins = act.activation(DTR[:, 1, :], bank(3, 3)[:, 0:16], ACT.Copy)
                elif p == 4:
                    for r, h in halves:
                        ins = act.activation(QK[:, r, h * 512:(h + 1) * 512], bank(4, 2 * r + h)[:, :], ACT.Copy)
                else:
                    for r, h in halves:
                        ins = act.activation(ZS[:, r, h * 512:(h + 1) * 512], bank(6, 2 * r + h)[:, :], ACT.Silu)
                ins.then_inc(set_free.sem, 1)

            def conv_tap3(layer, p, src, dst, first, count):
                act.wait_ge(set_free.sem, set_free.at(layer, p + 1))
                for j in range(count):
                    t = first + j
                    act.activation(dst[:, j, :], src[:, j, :], ACT.Identity, bias=cCB[:, t:t + 1],
                                   scale=cCW[:, 3, t:t + 1]).then_inc(cv_in.sem, 1)

            def hg_out(layer, i, p):
                h, t = divmod(i, 2)
                act.wait_ge(hg_o.sem, hg_o.at(layer, i + 1))
                o = work(p, 2)[:, 0:P]
                act.activation(LF[:, t, h * P:(h + 1) * P], o, ACT.Copy)
                act.activation(HJ[:, :], o, ACT.Square, accum_out=SSQ[:, t * 4 + h:t * 4 + h + 1]
                               ).then_inc(hg_oe.sem, 1)

            for n in range(W_SLOTS):
                hi_split(0, n, n, 0)
            with act.Fori(0, DEPTH) as layer:
                link.start(layer)
                h_chunk(layer, 0, 0)
                for p in range(FF0):
                    for kt in range(KT):
                        n = p * KT + kt
                        if n >= W_SLOTS:
                            hi_split(layer, n, n, n // RAW_SLOTS, width(p))
                        at = (p, kt)
                        if p == 0 and kt in (5, 9, 13):
                            h_chunk(layer, 0, kt // 4)
                        if kt == 2 and 1 <= p <= 7:
                            evacuate(layer, p - 1)
                        if at == (1, 4):
                            act.wait_ge(hg_f.sem, hg_f.at(layer, 4))
                            act.activation(E[:, :, :], EQ[:, :, :], ACT.Ln).then_inc(hg_lnf.sem, 1)
                        if at == (1, 9):
                            act.wait_ge(hg_logT.sem, hg_logT.at(layer, 1))
                            act.activation(LF[:, 0, :], work(1, 0)[:, :], ACT.Copy)
                            act.activation(LF[:, 1, :], work(1, 1)[:, :], ACT.Copy).then_inc(hg_log.sem, 1)
                        if p in (2, 3) and kt in HG_X1:
                            i = (p - 2) * 4 + HG_X1.index(kt)
                            act.wait_ge(hg_x.sem, hg_x.at(layer, i + 1))
                            if i:
                                act.wait_ge(hg_s.sem, hg_s.at(layer, i))
                            act.activation(E[:, 0:4, :], work(p, 0)[:, :], ACT.Exp)
                            act.activation(E[:, 4:8, :], work(p, 1)[:, :], ACT.Exp).then_inc(hg_e.sem, 1)
                        if (p, kt - 1) in HG_O:
                            hg_out(layer, HG_O.index((p, kt - 1)), p)
                        if at == (3, 3):
                            conv_tap3(layer, 2, U, CV, 0, 8)
                        if at == (3, 13):
                            act.wait_ge(cv_done.sem, cv_done.at(layer, 1))
                            act.activation(U[:, :, :], CV[:, :, :], ACT.Silu).then_inc(cv_act.sem, 1)
                        if at == (4, 3):
                            conv_tap3(layer, 3, BU, CB2, 8, 4)
                        if at == (4, 5):
                            act.wait_ge(dt_abs.sem, dt_abs.at(layer, 1))
                            act.activation(DTW[1][:, :], DTW[1][:, :], ACT.Exp, scale=-1.0).then_inc(dt_exp.sem, 1)
                        if at == (4, 6):
                            act.wait_ge(dt_u.sem, dt_u.at(layer, 1))
                            act.activation(DTW[3][:, :], DTW[2][:, :], ACT.Ln).then_inc(dt_ln.sem, 1)
                            rsqrt(layer, 1, 8)
                        if at == (4, 8):
                            act.wait_ge(cv_done.sem, cv_done.at(layer, 2))
                            act.activation(BC[:, :, :], CB2[:, :, :], ACT.Silu).then_inc(cv_act.sem, 1)
                        if at == (4, 9):
                            for r in range(2):
                                act.wait_ge(xs_T.sem, xs_T.at(layer, r + 1))
                                for b in range(2):
                                    ins = act.activation(XS[:, r, b * 512:(b + 1) * 512],
                                                         work(4, 2 * r + b)[:, :], ACT.Copy)
                                ins.then_inc(xs_rows.sem, 1)
                        if at == (4, 11):
                            t2_chunk(layer, 1, 4, (0, 1), 4, 0, cHGW)
                        if at == (4, 12):
                            act.wait_ge(dt_rows.sem, dt_rows.at(layer, 1))
                            act.activation(DTC[:, :, :, :], work(4, 2)[:, 0:64], ACT.Copy).then_inc(dt_ready.sem, 1)
                        if p == 5 and kt in M_ARG:
                            i = M_ARG.index(kt)
                            act.wait_ge(m_arg.sem, m_arg.at(layer, i + 1))
                            act.activation(MW[:, i % 2, :, :], MW[:, i % 2, :, :], ACT.Exp).then_inc(m_exp.sem, 1)
                        if at == (6, 4):
                            act.wait_ge(r_T.sem, r_T.at(layer, 1))
                            act.activation(RQT[:, 0:2, :], work(6, 0)[:, :], ACT.Copy)
                            act.activation(RQT[:, 2:4, :], work(6, 1)[:, :], ACT.Copy)
                            act.activation(RKT[:, 0:2, :], work(6, 2)[:, :], ACT.Copy)
                            act.activation(RKT[:, 2:4, :], work(6, 3)[:, :], ACT.Copy).then_inc(r_Te.sem, 1)
                        if at == (6, 9):
                            act.wait_ge(r_o.sem, r_o.at(layer, 1))
                            for t in range(2):
                                act.activation(RO[:, t, :], work(6, t)[:, :], ACT.Copy)
                                for h in range(4):
                                    ins = act.activation(JUNK[:, 4 * t + h, :], work(6, t)[:, h * P:(h + 1) * P], ACT.Square,
                                                         accum_out=SSQ[:, t * 4 + h:t * 4 + h + 1])
                            ins.then_inc(r_oe.sem, 1)
                            rsqrt(layer, 2, 8)
                        if at == (6, 14):
                            t2_chunk(layer, 2, 6, (2, 3), 0, 4)
                        if at == (7, 4):
                            act.wait_ge(m_z.sem, m_z.at(layer, 1))
                            for b in range(4):
                                ins = act.activation(ZS[:, b // 2, (b % 2) * 512:(b % 2 + 1) * 512], XS[:, b // 2, (b % 2) * 512:(b % 2 + 1) * 512],
                                                     ACT.Square, accum_out=SSQ[:, b:b + 1])
                            ins.then_inc(m_sq.sem, 1)
                            rsqrt(layer, 3, 4)
                        if at == (7, 9):
                            t2_chunk(layer, 3, 7, (0, 1, 2, 3), 8, 8, cMNW)
                        if at == (7, 13):
                            act.wait_ge(t2_ready.sem, t2_ready.at(layer, 16))
                            gate_rows(layer, 1, 7, range(4))
                for n in range(FF0 * KT, FF0 * KT + W_SLOTS):
                    hi_split(layer, n, n, n // RAW_SLOTS)
                layer_norm_rows(layer, 0)
                h_chunk(layer, 1, 0)
                with act.Fori(0, GROUPS) as g:
                    def relu_evac(s):
                        act.wait_ge(unit_done.sem, unit_done.at(layer, KT * (FF0 + g * 4 + s + 1)))
                        k0 = g * 8 + 4 * s
                        if s == 0:
                            act.wait_ge(x_add.sem, x_add.at(layer, 8 + g * 8))
                        for b in range(5):
                            if b < 4:
                                if b >= 2 or s == 1:
                                    act.wait_ge(ff_sq.sem, ff_sq.at(layer, k0 + b - 1))
                                act.activation(R[:, b % 2, :], bank(FF0 + s, b)[:, :], ACT.Relu
                                               ).then_inc(ff_relu.sem, 1)
                            if b >= 1:
                                act.wait_ge(ff_sq.sem, ff_sq.at(layer, k0 + b))
                                kt = 8 * s + 2 * (b - 1)
                                act.activation(T2h[:, kt:kt + 2, :], SQ[:, (b - 1) % 2, :], ACT.Copy
                                               ).then_inc(ff_hi.sem, 1)

                    def split(m):
                        hi_split(layer, g * 64 + FF0 * KT + m, m, g * 8 + FF0 * KT // RAW_SLOTS + m // RAW_SLOTS)

                    for m in range(W_SLOTS, 4 * KT):
                        s, kt = divmod(m, KT)
                        split(m)
                        if s == 0 and kt in (5, 9, 13):
                            with act.If(g < 1):
                                h_chunk(layer, 1, kt // 4)
                        if kt == 2 and s in (1, 2):
                            relu_evac(s - 1)
                        if m in (36, 63):
                            with act.If(g < 1):
                                gate_rows(layer, 2 if m < 63 else 3, FF0 + s, (0, 1) if m < 63 else (2, 3))
                    with act.If(g + GROUPS * layer < GROUPS * DEPTH - 1):
                        for m in range(4 * KT, 4 * KT + W_SLOTS):
                            split(m)
                layer_norm_rows(layer, 1)
                link.end("act")

        @block.vector
        def _(dve):
            link = Order(dve, order["dve"])
            tt, ts, stt = dve.tensor_tensor, dve.tensor_scalar, dve.scalar_tensor_tensor

            def ada_mul(in_sem, in_count, mac_count, sums, w, k):
                dve.wait_ge(in_sem, in_count)
                if k == 0:
                    if sums is not None:
                        dve.wait_ge(ada_sum.sem, sums)
                    ins = ts(ACC[:, :], w, CT[:, 0:1], None, ALU.mult)
                else:
                    dve.wait_ge(ada_mac.sem, mac_count)
                    ins = stt(ACC[:, :], w, CT[:, k:k + 1], ACC[:, :], ALU.mult, ALU.add)
                ins.then_inc(ada_mac.sem, 1)

            def ada_out(sum_count, col, bank_ap):
                dve.wait_ge(ada_sum.sem, sum_count)
                tt(ADA[:, ds(col, 8)], bank_ap[:, 0:8], PT[:, ds(col, 8)], ALU.add).then_inc(ada_cols.sem, 1)

            dve.wait_ge(pro_act.sem, 1)
            link(ts(E16[:, :], E16[:, :], 1.0, None, ALU.add))
            link(dve.reciprocal(E16[:, :], E16[:, :]))
            link(tt(CT[:, :], E16[:, :], PT[:, T_C:T_C + KT], ALU.mult))
            dve.wait_ge(pro_in.sem, 16 * 7)
            dve.tensor_copy(LM[:, :], LMs[:, :])
            link(dve.tensor_copy(POSF[:, :], POSI[:, :]))
            for r in range(2):
                ins = ts(ANG[:, r, :], FREQ[:, :], POSF[:, r:r + 1], None, ALU.mult)
            dve.wait_ge(pro_pt.sem, 1)
            lb0, lb1 = PT[:, T_LB:T_LB + 4], PT[:, T_LB + 4:T_LB + 8]
            link(tt(LMX[:, :], lb0, lb1, ALU.max))
            tt(LX[:, 0:4], lb0, LMX[:, :], ALU.subtract)
            tt(LX[:, 4:8], lb1, LMX[:, :], ALU.subtract).then_inc(pro_dve.sem, 1)
            link(ts(RND[:, :, :], ANG[:, :, :], 1.0 / TWO_PI, MAGIC, ALU.mult, ALU.add))
            link(ts(RND[:, :, :], RND[:, :, :], MAGIC, None, ALU.subtract))
            for part in (C1, C2, C3):
                link(stt(ANG[:, :, :], RND[:, :, :], -part, ANG[:, :, :], ALU.mult, ALU.add))
            ts(ANG[:, :, :], ANG[:, :, :], 3.1415925, -3.1415925, ALU.min, ALU.max).then_inc(pro_dve.sem, 1)
            dve.wait_ge(pro_act.sem, 5)
            ts(NA[:, :], AL[:, :], -1.0, None, ALU.mult)
            link(tt(LMX[:, :], LX[:, 0:4], LX[:, 4:8], ALU.add))
            link(dve.reciprocal(LMX[:, :], LMX[:, :]))
            dve.memset(LBT[:, 0:4], 0.0)
            link(tt(LBT[:, 4:8], LX[:, 4:8], LMX[:, :], ALU.mult))
            ts(OML[:, :], LBT[:, :], -1.0, 1.0, ALU.mult, ALU.add)
            link(tt(S2[:, :, :], S2[:, :, :], S2[:, :, :], ALU.mult))
            link(ts(COS[:, :, :], S2[:, :, :], -2.0, 1.0, ALU.mult, ALU.add))
            for a in range(64):
                ada_mul(raw_in[a % RAW_SLOTS].sem, 16 * (a // RAW_SLOTS + 1), a + 2, a // 16 if a >= 16 else None,
                        RAW[:, a % RAW_SLOTS, :], a % 16)
                if a >= 64 - RAW_SLOTS:
                    dve.wait_ge(ada_mac.sem, a + 3)
                    dve.memset(IDLE[:, 3:4], 0.0).then_inc(lo_done.sem, 1)
                if a % 16 == 15:
                    ada_out(a // 16 + 1, (a // 16) * 8, PB[4])

            def lo_split(layer, n, m, w=UW):
                dve.wait_ge(hi_done.sem, hi_done.at(layer, n + 1))
                tt(WL[:, m % W_SLOTS, 0:w], RAW[:, m % RAW_SLOTS, 0:w], WH[:, m % W_SLOTS, 0:w].bitcast(F32),
                   ALU.subtract).then_inc(lo_done.sem, 1)

            def t_lo(tt_, hi_sig, hi_count, k, hi, lo, ready):
                dve.wait_ge(hi_sig.sem, hi_count)
                tt(lo, tt_[:, k % 4, :], hi.bitcast(F32), ALU.subtract).then_inc(ready.sem, 1)

            def h_chunk(layer, s, ch):
                for kt in range(4 * ch, 4 * ch + 4):
                    t_lo(TX, hT_hi, hT_hi.at(layer, 16 * s + kt + 1), kt, HTh[:, kt, :], HTl[:, kt, :], hT_ready)

            def t2_chunk(layer, which, kt0, count0, n):
                for i in range(n):
                    t_lo(TM[which], t2_hi, t2_hi.at(layer, count0 + i + 1), count0 + i, T2h[:, kt0 + i, :],
                         T2l[:, kt0 + i, :], t2_ready)

            def newton(layer, k, cols):
                dve.wait_ge(rs_act.sem, rs_act.at(layer, k))
                link(tt(RA[:, 0:cols], RR[:, 0:cols], RR[:, 0:cols], ALU.mult))
                link(tt(RA[:, 0:cols], RA[:, 0:cols], RV[:, 0:cols], ALU.mult))
                link(ts(RA[:, 0:cols], RA[:, 0:cols], -0.5, 1.5, ALU.mult, ALU.add))
                return tt(RR[:, 0:cols], RR[:, 0:cols], RA[:, 0:cols], ALU.mult)

            def rms(layer, k, cols, width_):
                ts(RV[:, 0:cols], SSQ[:, 0:cols], 1.0 / width_, RMS_EPS, ALU.mult, ALU.add).then_inc(rs_in.sem, 1)
                newton(layer, k, cols).then_inc(rs_out.sem, 1)

            def row_stats(layer, chunks, adds):
                dve.wait_ge(x_add.sem, adds)
                for r in range(2):
                    for ch in chunks:
                        ins = dve.bn_stats(BN[:, r, ch, :], X[:, r, ch * 512:(ch + 1) * 512])
                return ins

            def layer_norm_rows(layer, s, stats):
                link(stats)
                dve.memset(IDLE[:, 2:3], 0.0)
                dve.bn_aggr(MV[:, 0, :], BN[:, 0, :, :].rearrange("p a b -> p (a b)"))
                link(dve.bn_aggr(MV[:, 1, :], BN[:, 1, :, :].rearrange("p a b -> p (a b)")))
                ts(RV[:, 0:2], MV[:, :, 1], LN_EPS, None, ALU.add).then_inc(rs_in.sem, 1)
                link(newton(layer, 4 + s, 2))
                stt(NMR[:, :], MV[:, :, 0], -1.0, RR[:, 0:2], ALU.mult, ALU.mult).then_inc(rs_out.sem, 1)
                dve.wait_ge(ln_gb_in.sem, ln_gb_in.at(layer, 32 * (s + 1)))
                for ch in range(4):
                    dve.wait_ge(ln_norm.sem, ln_norm.at(layer, 4 * s + ch + 1))
                    xc = X[:, :, ch * 512:(ch + 1) * 512]
                    tt(xc, xc, bc(LNG[:, ch * 512:(ch + 1) * 512].unsqueeze(1), [P, 2, 512]), ALU.mult
                       ).then_inc(ln_mul.sem, 1)

            def gate_y(layer, p, k, half, passes, ready):
                dve.wait_ge(unit_done.sem, passes)
                dve.wait_ge(g_ready.sem, g_ready.at(layer, ready))
                for b in range(4):
                    if not (isinstance(k, int) and k + b < 2):
                        dve.wait_ge(x_add.sem, x_add.at(layer, k + b - 1))
                    col = half * UW + (b % 2) * 512
                    tt(R[:, b % 2, :], bank(p, b)[:, :], GB[:, col:col + 512], ALU.mult).then_inc(gated.sem, 1)

            def sub_layer_cols(layer, s):
                a0 = layer * 96 + 48 * s
                ts(SC[:, s, :], ADA[:, ds(a0 + 16, 16)], 1.0, None, ALU.add)
                dve.tensor_copy(SH[:, s, :], ADA[:, ds(a0, 16)]).then_inc(cols_set.sem, 1)

            def gate_cols(layer, k, a0, c0, n):
                ts(GC[:, c0:c0 + n], ADA[:, ds(layer * 96 + a0 + c0, n)], 1.0, None, ALU.add).then_inc(g_cols.sem, 1)

            def conv(layer, src, dst, j, t, last):
                dve.wait_ge(cv_in.sem, cv_in.at(layer, t + 1))
                for tap in (2, 1, 0):
                    sh = 3 - tap
                    ins = stt(dst[:, j, sh:SEQ], src[:, j, 0:SEQ - sh], cCW[:, tap, t:t + 1], dst[:, j, sh:SEQ],
                              ALU.mult, ALU.add)
                    if tap:
                        link(ins)
                if last:
                    ins.then_inc(cv_done.sem, 1)

            def hg_mask(layer, i, p):
                dve.wait_ge(hg_s.sem, hg_s.at(layer, i + 1))
                if i % 2:
                    if i > 1:
                        dve.wait_ge(hg_o.sem, hg_o.at(layer, i - 1))
                    dve.tensor_copy(SX[:, :], work(p, 0)[:, 0:P]).then_inc(hg_sx.sem, 1)
                for b in range(2):
                    ins = tt(MS[:, 4 * b:4 * b + 4, :], work(p, 2 + b)[:, :].rearrange("p (l i) -> p l i", i=P),
                             LM[:, b * 512:(b + 1) * 512].rearrange("p (l i) -> p l i", i=P), ALU.mult)
                link(ins)
                if i:
                    dve.wait_ge(hg_o.sem, hg_o.at(layer, i))
                dve.tensor_reduce(SM[:, :], MS[:, :, :].rearrange("p l i -> p i l"), AX.X, ALU.add
                                  ).then_inc(hg_sm.sem, 1)

            for n in range(W_SLOTS):
                lo_split(0, n, n)
            with dve.Fori(0, DEPTH) as layer:
                link.start(layer)
                dve.wait_ge(ada_cols.sem, ada_cols.at(layer, 0))
                dve.tensor_copy(cHGW[:, :], PT[:, ds(layer * 4 + T_HGW, 4)])
                dve.tensor_copy(cCB[:, :], PT[:, ds(layer * 12 + T_CB, 12)])
                dve.tensor_copy(cMNW[:, :], PT[:, ds(layer * 8 + T_MNW, 8)])
                dve.tensor_copy(cCW[:, :, :], PT[:, ds(layer * 48 + T_CW, 48)])
                dve.tensor_copy(cLB[:, :], LBT[:, ds(layer * 4, 4)])
                dve.tensor_copy(cOML[:, :], OML[:, ds(layer * 4, 4)])
                dve.tensor_copy(cMD[:, :], MD[:, ds(layer * 16, 16)])
                dve.tensor_copy(cDTB[:, :], DTB[:, ds(layer, 1)])
                dve.tensor_copy(cNA[:, :], NA[:, ds(layer, 1)])
                sub_layer_cols(layer, 0)
                h_chunk(layer, 0, 0)
                for p in range(FF0):
                    for kt in range(KT):
                        n = p * KT + kt
                        at = (p, kt)
                        if n >= W_SLOTS:
                            lo_split(layer, n, n, width(p))
                        if p == 0 and kt in (5, 9, 13):
                            h_chunk(layer, 0, kt // 4)
                        for a in ada_units(n, 24, 6):
                            ada_mul(ada_in[a % 2].sem, ada_in[0].at(layer, 16 * (a // 2 + 1)), ada_mac.at(layer, a),
                                    ada_sum.at(layer, a // 16), ADR[:, a % 2, :], a % 16)
                        if ada_due(n, 24, 6) is not None:
                            half = ada_due(n, 24, 6)
                            ada_out(ada_sum.at(layer, half + 1), layer * 96 + (4 + half) * 8,
                                    work(p, ada_bank(p)))
                        if at == (1, 3):
                            dve.wait_ge(set_free.sem, set_free.at(layer, 1))
                            for h in range(4):
                                fh = EQ[:, 2 * h:2 * h + 2, :]
                                ts(fh, fh, cOML[:, h:h + 1], cLB[:, h:h + 1], ALU.mult, ALU.add
                                   ).then_inc(hg_f.sem, 1)
                            dve.wait_ge(hg_f.sem, hg_f.at(layer, 4))
                            ts(KTt[:, :, :], EQ[:, :, :], -1.0, 1.0, ALU.mult, ALU.add).then_inc(hg_k.sem, 1)
                        if p in (2, 3) and kt in HG_X1:
                            i = (p - 2) * 4 + HG_X1.index(kt)
                            h, t = divmod(i, 2)
                            dve.wait_ge(hg_e.sem, hg_e.at(layer, i + 1))
                            tt(EQ[:, :, :], E[:, :, :], bc(QT[:, h, t * P:(t + 1) * P].unsqueeze(1), [P, 8, P]),
                               ALU.mult).then_inc(hg_eq.sem, 1)
                        if p in (2, 3) and kt in HG_M:
                            hg_mask(layer, (p - 2) * 4 + HG_M.index(kt), p)
                        if p == 3 and 3 <= kt <= 10:
                            conv(layer, U, CV, kt - 3, kt - 3, kt == 10)
                        if p == 4 and 3 <= kt <= 6:
                            conv(layer, BU, CB2, kt - 3, kt + 5, kt == 6)
                        if at == (4, 4):
                            dve.wait_ge(dt_T.sem, dt_T.at(layer, 1))
                            link(ts(DTW[0][:, :], work(4, 3)[0:16, 0:SEQ], cDTB[:, 0:1], None, ALU.add))
                            stt(DTW[1][:, :], DTW[0][:, :], -1.0, DTW[0][:, :], ALU.mult, ALU.max
                                ).then_inc(dt_abs.sem, 1)
                        if at == (4, 5):
                            dve.wait_ge(dt_exp.sem, dt_exp.at(layer, 1))
                            ts(DTW[2][:, :], DTW[1][:, :], 1.0, None, ALU.add).then_inc(dt_u.sem, 1)
                        if at == (4, 6):
                            dve.wait_ge(hg_oe.sem, hg_oe.at(layer, 8))
                            rms(layer, 1, 8, P)
                        if at == (4, 7):
                            dve.wait_ge(dt_ln.sem, dt_ln.at(layer, 1))
                            link(ts(DTW[2][:, :], DTW[2][:, :], -1.0, 1e-30, ALU.add, ALU.add))
                            link(dve.reciprocal(DTW[2][:, :], DTW[2][:, :]))
                            link(stt(DTW[3][:, :], DTW[3][:, :], 1e-30, DTW[2][:, :], ALU.add, ALU.mult))
                            link(tt(DTW[3][:, :], DTW[3][:, :], DTW[1][:, :], ALU.mult))
                            link(stt(DTT[:, :], DTW[0][:, :], 0.0, DTW[3][:, :], ALU.max, ALU.add))
                            link(ts(DTW[0][:, :], DTT[:, :], cNA[:, 0:1], None, ALU.mult))
                            dve.tensor_tensor_scan(CUM[:, :], bc(ones[0:16, :], [16, SEQ]), DTW[0][:, :], 0.0,
                                                   ALU.mult, ALU.add).then_inc(dt_cum.sem, 1)
                        if at == (4, 11):
                            t2_chunk(layer, 1, 4, 0, 4)
                        if at in ((4, 13), (4, 14)):
                            gr = kt - 13
                            dve.wait_ge(m_s.sem, m_s.at(layer, gr + 1))
                            tt(SB[:, gr, :], work(4, 3 if gr == 0 else 0)[:, 0:384], K[:, K_TRI:K_TRI + 384],
                               ALU.mult).then_inc(m_sm.sem, 1)
                        if p == 5 and kt in M_MUL:
                            i = M_MUL.index(kt)
                            dve.wait_ge(m_exp.sem, m_exp.at(layer, i + 1))
                            if i == 0:
                                dve.wait_ge(m_sm.sem, m_sm.at(layer, 2))
                            tt(MW[:, i % 2, :, :], MW[:, i % 2, :, :],
                               bc(SB[:, i // 4, :].unsqueeze(1), [P, 2, 384]), ALU.mult).then_inc(m_m.sem, 1)
                        if at in ((5, 11), (5, 15)):
                            gr = 0 if kt == 11 else 1
                            dve.wait_ge(m_y.sem, m_y.at(layer, 4 * gr + 4))
                            dve.wait_ge(xsd_ready.sem, xsd_ready.at(layer, 1))
                            for r in range(2):
                                xs = XS[:, r, gr * 512:(gr + 1) * 512]
                                ins = tt(xs, xs, work(5, r)[:, :], ALU.add)
                            ins.then_inc(m_ye.sem, 1)
                        if p == 5 and kt in M_ARG:
                            i = M_ARG.index(kt)
                            dve.wait_ge(m_cum.sem, m_cum.at(layer, i + 1))
                            if i == 0:
                                dve.wait_ge(dt_ready.sem, dt_ready.at(layer, 1))
                            if i >= 2:
                                dve.wait_ge(m_y.sem, m_y.at(layer, i - 1))
                            for e in range(2):
                                hd = 2 * i + e
                                cb = work(5, 2 + i % 2)[:, e * SEQ:(e + 1) * SEQ]
                                ts(MW[:, i % 2, e, 0:SEQ], cb, DTC[:, 0, 1, hd:hd + 1], 0.0, ALU.subtract, ALU.min)
                                ins = ts(MW[:, i % 2, e, SEQ:384], cb[:, P:SEQ], DTC[:, 1, 1, hd:hd + 1], 0.0,
                                         ALU.subtract, ALU.min)
                            ins.then_inc(m_arg.sem, 1)
                        if at == (6, 6):
                            for h in range(4):
                                dve.wait_ge(r_s.sem, r_s.at(layer, h // 2 + 1))
                                dg = K_DG + h * SEQ
                                tt(SR[:, h, 0:SEQ], work(6, h)[:, 0:SEQ], K[:, dg:dg + SEQ], ALU.mult)
                                tt(SR[:, h, SEQ:384], work(6, h)[:, SEQ:384], K[:, dg:dg + P], ALU.mult
                                   ).then_inc(r_sm.sem, 1)
                        if at == (6, 9):
                            dve.wait_ge(r_oe.sem, r_oe.at(layer, 1))
                            rms(layer, 2, 8, P)
                        if at == (6, 14):
                            t2_chunk(layer, 2, 0, 4, 4)
                        if at == (7, 3):
                            dve.wait_ge(set_free.sem, set_free.at(layer, 7))
                            dve.wait_ge(m_ye.sem, m_ye.at(layer, 2))
                            for r in range(2):
                                ins = tt(XS[:, r, :], XS[:, r, :], ZS[:, r, :], ALU.mult)
                            ins.then_inc(m_z.sem, 1)
                        if at == (7, 4):
                            dve.wait_ge(m_sq.sem, m_sq.at(layer, 1))
                            rms(layer, 3, 4, 512)
                            dve.wait_ge(rs_out.sem, rs_out.at(layer, 3))
                            for b in range(4):
                                xs = XS[:, b // 2, (b % 2) * 512:(b % 2 + 1) * 512]
                                ins = ts(xs, xs, RR[:, b:b + 1], None, ALU.mult)
                            ins.then_inc(m_rows.sem, 1)
                        if at == (7, 9):
                            t2_chunk(layer, 3, 8, 8, 8)
                        if at == (7, 11):
                            dve.wait_ge(ada_cols.sem, ada_cols.at(layer, 2))
                            gate_cols(layer, 1, 32, 0, 16)
                        if at == (8, 2):
                            gate_y(layer, 7, 0, 0, unit_done.at(layer, KT * (8)), 1)
                        if at == (8, 8):
                            row_stats(layer, (0, 1), x_add.at(layer, 4))
                for n in range(FF0 * KT, FF0 * KT + W_SLOTS):
                    lo_split(layer, n, n)
                dve.wait_ge(ada_cols.sem, ada_cols.at(layer, 6))
                sub_layer_cols(layer, 1)
                gate_y(layer, 8, 4, 1, unit_done.at(layer, KT * (9)), 1)
                layer_norm_rows(layer, 0, row_stats(layer, (2, 3), x_add.at(layer, 8)))
                h_chunk(layer, 1, 0)
                with dve.Fori(0, GROUPS) as g:
                    def group(ada):
                        for m in range(4 * KT):
                            s, kt = divmod(m, KT)
                            if m >= W_SLOTS:
                                lo_split(layer, g * 64 + FF0 * KT + m, m)
                            if s == 0 and kt in (5, 9, 13):
                                with dve.If(g < 1):
                                    h_chunk(layer, 1, kt // 4)
                            for a in ada_units(m, 32, 2) if ada else ():
                                ada_mul(ada_in[a % 2].sem, ada_in[0].at(layer, g * 256 + 16 * (48 + a // 2 + 1)),
                                        ada_mac.at(layer, g * 32 + 96 + a), ada_sum.at(layer, g * 2 + 6 + a // 16),
                                        ADR[:, a % 2, :], a % 16)
                            if ada and ada_due(m, 32, 2) is not None:
                                half = ada_due(m, 32, 2)
                                ada_out(ada_sum.at(layer, g * 2 + 7 + half),
                                        ((layer * 12 + g * 2 + 10 + half) % 24) * 8, work(FF0 + s, 3))
                            if s in (1, 2) and kt == 2:
                                for b in range(4):
                                    k = g * 8 + 4 * (s - 1) + b
                                    dve.wait_ge(ff_hi.sem, ff_hi.at(layer, k + 1))
                                    t = 8 * (s - 1) + 2 * b
                                    tt(T2l[:, t:t + 2, :], SQ[:, b % 2, :].rearrange("p (a b) -> p a b", a=2),
                                       T2h[:, t:t + 2, :].bitcast(F32), ALU.subtract).then_inc(ff_ready.sem, 1)
                            if m == 2:
                                with dve.If(g > 0):
                                    gate_y(layer, FF0 + 3, g * 8 + 4, 1, unit_done.at(layer, KT * (g * 4 + FF0)), 3)
                            if m == 34 or m == 63:
                                with dve.If(g < 1):
                                    i = 0 if m == 34 else 1
                                    dve.wait_ge(ada_cols.sem, ada_cols.at(layer, 7 + i))
                                    gate_cols(layer, 2 + i, 80, 8 * i, 8)
                            if m == 50:
                                gate_y(layer, FF0 + 2, g * 8 + 8, 0, unit_done.at(layer, KT * (g * 4 + FF0 + 3)), 2)

                    with dve.If(g + 2 * layer < 3):
                        group(True)
                    with dve.Else():
                        group(False)
                    with dve.If(g + GROUPS * layer < GROUPS * DEPTH - 1):
                        for m in range(4 * KT, 4 * KT + W_SLOTS):
                            lo_split(layer, g * 64 + FF0 * KT + m, m)
                gate_y(layer, FF0 + 3, 36, 1, unit_done.at(layer, KT * (NPASS)), 3)
                layer_norm_rows(layer, 1, row_stats(layer, (0, 1, 2, 3), x_add.at(layer, 40)))
                link.end("dve")

        @block.tensor
        def _(pe):
            mm, tr = pe.matmul, pe.transpose

            def ada_sums(mac_count, bank_ap):
                pe.wait_ge(ada_mac.sem, mac_count)
                for i in range(8):
                    ins = mm(bank_ap[:, i:i + 1], ACC[:, i * P:(i + 1) * P], ones, start=True, stop=True)
                ins.then_inc(ada_sum.sem, 1)

            pe.wait_ge(pro_st.sem, 16 * 9)
            for j, rows in enumerate((P, P, 104)):
                ins = tr(PB[0][:, j * P:j * P + rows], ST[0:rows, j, :], ident[0:rows, 0:rows])
            ins.then_inc(pro_T.sem, 1)
            for q in range(4):
                if q:
                    pe.wait_ge(ada_cols.sem, q)
                else:
                    pe.wait_ge(pro_in.sem, 16 * 7)
                ada_sums(16 * (q + 1) + 2, PB[4])
            pe.wait_ge(ada_cols.sem, 4)

            def x_transpose(layer, s, ch):
                pe.wait_ge(x_ready.sem, x_ready.at(layer, 4 * s + ch + 1) - 4)
                if ch >= 2:
                    pe.wait_ge(hT_hi.sem, hT_hi.at(layer, 16 * s + 4 * (ch - 1)))
                for b in (2 * ch, 2 * ch + 1):
                    for j in range(2):
                        for r in range(2):
                            kt = 2 * b + j
                            ins = tr(work(s * FF0, b % 4)[:, j * SEQ + r * P:j * SEQ + (r + 1) * P],
                                     X[:, r, kt * P:(kt + 1) * P], ident)
                    ins.then_inc(xT.sem, 1)

            def unit(layer, n, m, p, kt, left, kind, first, last):
                pe.wait_ge(lo_done.sem, lo_done.at(layer, n + 1))
                k = m % W_SLOTS
                lh, ll = left
                if kind == "rows":
                    for r in range(2):
                        rows = slice(r * P, (r + 1) * P)
                        for i, (a, w) in enumerate(((lh, WH), (lh, WL), (ll, WH))):
                            for h in range(2):
                                ins = mm(bank(p, 2 * r + h)[:, :], a[:, kt, rows], w[:, k, h * 512:(h + 1) * 512],
                                         start=first and i == 0, stop=last and i == 2)
                else:
                    tiles = 4 if kind == "bc" else 8
                    for j in range(tiles):
                        dst = bank(p, j // 2)[:, (j % 2) * SEQ:(j % 2 + 1) * SEQ]
                        cols = slice(j * P, (j + 1) * P)
                        for i, (a, w) in enumerate(((lh, WH), (ll, WH), (lh, WL))):
                            ins = mm(dst, w[:, k, cols], a[:, kt, :], start=first and i == 0 and j % 2 == 0,
                                     stop=last and i == 2, skip_group_check=True)
                    if kind == "bc":
                        for r in range(2):
                            for i, (a, w) in enumerate(((lh, WH), (lh, WL), (ll, WH))):
                                ins = mm(bank(p, 2 + r)[:, 0:16], a[:, kt, r * P:(r + 1) * P], w[:, k, 512:528],
                                         start=first and i == 0, stop=last and i == 2)
                ins.then_inc(unit_done.sem, 1)

            def hg_levels(layer, i, p):
                h, t = divmod(i, 2)
                f = LF[:, t, h * P:(h + 1) * P]
                if i % 2 == 0 and i:
                    pe.wait_ge(hg_sx.sem, hg_sx.at(layer, i // 2))
                mm(work(p, 0)[:, :], f, K[:, K_ML:K_ML + 512], start=True, stop=True)
                last = K_ML + (7 + t) * P
                mm(work(p, 1)[:, 0:384], f, K[:, K_ML + 512:K_ML + 896], start=True, stop=True)
                mm(work(p, 1)[:, 384:512], f, K[:, last:last + P], start=True, stop=True).then_inc(hg_x.sem, 1)

            def hg_scores(layer, i, p):
                h, t = divmod(i, 2)
                rows = slice(t * P, (t + 1) * P)
                pe.wait_ge(hg_ek.sem, hg_ek.at(layer, i + 1))
                if i and HG_O[i - 1][0] == p:
                    pe.wait_ge(hg_oe.sem, hg_oe.at(layer, i))
                for lv in range(7):
                    mm(work(p, 2 + lv // 4)[:, (lv % 4) * P:(lv % 4 + 1) * P], E[:, lv, :], EQ[:, lv, :],
                       start=True, stop=True)
                if t == 1:
                    mm(work(p, 0)[:, 0:P], CROSSK[:, :], EQ[:, 7, :], start=True, stop=True)
                mm(work(p, 3)[:, 384:512], KTt[:, h, rows], QT[:, h, rows], start=True, stop=True
                   ).then_inc(hg_s.sem, 1)

            def hg_output(layer, i, p):
                h, t = divmod(i, 2)
                cols = slice(h * P, (h + 1) * P)
                pe.wait_ge(hg_sm.sem, hg_sm.at(layer, i + 1))
                o = work(p, 2)[:, 0:P]
                ins = mm(o, SM[:, :], V[:, t, cols], start=True, stop=(t == 0))
                if t == 1:
                    ins = mm(o, SX[:, :], V[:, 0, cols], start=False, stop=True)
                ins.then_inc(hg_o.sem, 1)

            def rows_to_t2(src, bank_of, n):
                for j in range(n):
                    for r in range(2):
                        ins = tr(bank_of(j // 2)[:, (j % 2) * SEQ + r * P:(j % 2) * SEQ + (r + 1) * P],
                                 src[:, r, j * P:(j + 1) * P], ident)
                ins.then_inc(t2_T.sem, 1)

            def gate_broadcast(layer, k, p, kts):
                pe.wait_ge(g_cols.sem, g_cols.at(layer, k))
                for i, kt in enumerate(kts):
                    ins = mm(work(p, i // 4)[:, (i % 4) * P:(i % 4 + 1) * P], bc(GC[:, kt:kt + 1], [P, P]), ident,
                             start=True, stop=True)
                ins.then_inc(g_bc.sem, 1)

            with pe.Fori(0, DEPTH) as layer:
                for p in range(FF0):
                    kind = "bc" if p == 3 else "cols" if p in (0, 2) else "rows"
                    if p == 1:
                        pe.wait_ge(hT_hi.sem, hT_hi.at(layer, 16))
                    if p >= 2:
                        pe.wait_ge(set_free.sem, set_free.at(layer, p - 1))
                    if p == 3:
                        pe.wait_ge(hg_sm.sem, hg_sm.at(layer, 4))
                    if p == 4:
                        pe.wait_ge(hg_sm.sem, hg_sm.at(layer, 8))
                    if p == 5:
                        pe.wait_ge(m_sm.sem, m_sm.at(layer, 2))
                        pe.wait_ge(dt_ready.sem, dt_ready.at(layer, 1))
                    if p == 6:
                        pe.wait_ge(m_ye.sem, m_ye.at(layer, 2))
                        pe.wait_ge(ada_cols.sem, ada_cols.at(layer, 4))
                    if p == 7:
                        pe.wait_ge(t2_hi.sem, t2_hi.at(layer, 8))
                    if p == 8:
                        pe.wait_ge(g_ready.sem, g_ready.at(layer, 1))
                    for kt in range(KT):
                        n = p * KT + kt
                        at = (p, kt)
                        if p == 0 and kt in (0, 2, 6, 10):
                            x_transpose(layer, 0, (kt + 2) // 4)
                        if p == 0:
                            pe.wait_ge(hT_ready.sem, hT_ready.at(layer, kt + 1))
                        if at == (1, 8):
                            pe.wait_ge(hg_lnf.sem, hg_lnf.at(layer, 1))
                            for h in range(4):
                                for t in range(2):
                                    ins = tr(work(1, t)[:, h * P:(h + 1) * P], E[:, 2 * h + t, :], ident)
                            ins.then_inc(hg_logT.sem, 1)
                        if p in (2, 3) and kt in HG_X:
                            i = (p - 2) * 4 + HG_X.index(kt)
                            if i == 0:
                                pe.wait_ge(hg_log.sem, hg_log.at(layer, 1))
                            if i in (0, 4):
                                pe.wait_ge(set_free.sem, set_free.at(layer, p))
                            hg_levels(layer, i, p)
                        if p in (2, 3) and kt in HG_S:
                            hg_scores(layer, (p - 2) * 4 + HG_S.index(kt), p)
                        if at in HG_O:
                            if at == (4, 4):
                                pe.wait_ge(set_free.sem, set_free.at(layer, 4))
                            hg_output(layer, HG_O.index(at), p)
                        if at == (4, 3):
                            pe.wait_ge(set_free.sem, set_free.at(layer, 4))
                            for r in range(2):
                                ins = tr(work(4, 3)[0:16, r * P:(r + 1) * P], DTR[:, r, :], ident)
                            ins.then_inc(dt_T.sem, 1)
                        if at == (4, 8):
                            pe.wait_ge(cv_act.sem, cv_act.at(layer, 1))
                            pe.wait_ge(hg_oe.sem, hg_oe.at(layer, 8))
                            for r in range(2):
                                for j in range(8):
                                    ins = tr(work(4, 2 * r + j // 4)[:, (j % 4) * P:(j % 4 + 1) * P],
                                             U[:, j, r * P:(r + 1) * P], ident)
                                ins.then_inc(xs_T.sem, 1)
                        if at == (4, 10):
                            pe.wait_ge(xs_rows.sem, xs_rows.at(layer, 1))
                            pe.wait_ge(hg_rows.sem, hg_rows.at(layer, 1))
                            rows_to_t2(LF, lambda b: work(4, b), 4)
                        if at == (4, 11):
                            pe.wait_ge(xs_rows.sem, xs_rows.at(layer, 2))
                            pe.wait_ge(dt_cum.sem, dt_cum.at(layer, 1))
                            for r in range(2):
                                for w, src in enumerate((DTT, CUM)):
                                    c0 = (2 * r + w) * 16
                                    ins = mm(work(4, 2)[:, c0:c0 + 16], src[:, r * P:(r + 1) * P],
                                             ident[0:16, 0:16], start=True, stop=True)
                            ins.then_inc(dt_rows.sem, 1)
                        if at in ((4, 12), (4, 13)):
                            gr = kt - 12
                            if gr == 0:
                                pe.wait_ge(cv_act.sem, cv_act.at(layer, 2))
                            else:
                                pe.wait_ge(t2_hi.sem, t2_hi.at(layer, 4))
                            b_ = work(4, 3 if gr == 0 else 0)
                            mm(b_[:, 0:SEQ], BC[:, gr, 0:P], BC[:, 2 + gr, :], start=True, stop=True)
                            mm(b_[:, SEQ:384], BC[:, gr, P:SEQ], BC[:, 2 + gr, P:SEQ], start=True, stop=True
                               ).then_inc(m_s.sem, 1)
                        if p == 5 and kt in M_CUM:
                            i = M_CUM.index(kt)
                            if i == 0:
                                pe.wait_ge(set_free.sem, set_free.at(layer, 5))
                            if i >= 2:
                                pe.wait_ge(m_arg.sem, m_arg.at(layer, i - 1))
                            for e in range(2):
                                hd = 2 * i + e
                                ins = mm(work(5, 2 + i % 2)[:, e * SEQ:(e + 1) * SEQ],
                                         bc(ident[0:16, hd:hd + 1], [16, P]), CUM[:, :], start=True, stop=True)
                            ins.then_inc(m_cum.sem, 1)
                        if p == 5 and kt in M_Y:
                            i = M_Y.index(kt)
                            pe.wait_ge(m_m.sem, m_m.at(layer, i + 1))
                            if i == 0:
                                pe.wait_ge(xd_ready.sem, xd_ready.at(layer, 1))
                            if i == 4:
                                pe.wait_ge(m_ye.sem, m_ye.at(layer, 1))
                            for e in range(2):
                                hd = 2 * i + e
                                v = slice(hd * 64, (hd + 1) * 64)
                                y = slice((hd % 8) * 64, (hd % 8 + 1) * 64)
                                mm(work(5, 0)[:, y], MW[:, i % 2, e, 0:P], XD[:, 0, v], start=True, stop=True)
                                mm(work(5, 1)[:, y], MW[:, i % 2, e, P:SEQ], XD[:, 0, v], start=True, stop=False)
                                ins = mm(work(5, 1)[:, y], MW[:, i % 2, e, SEQ:384], XD[:, 1, v], start=False,
                                         stop=True)
                            ins.then_inc(m_y.sem, 1)
                        if at == (6, 3):
                            pe.wait_ge(set_free.sem, set_free.at(layer, 6))
                            pe.wait_ge(r_rot.sem, r_rot.at(layer, 1))
                            for w in range(2):
                                for h in range(4):
                                    for t in range(2):
                                        c0 = w * 512 + h * P
                                        ins = tr(work(6, 2 * w + h // 2)[:, (h % 2) * SEQ + t * P:
                                                                         (h % 2) * SEQ + (t + 1) * P],
                                                 QK[:, t, c0:c0 + P], ident)
                            ins.then_inc(r_T.sem, 1)
                        if at == (6, 5):
                            pe.wait_ge(r_Te.sem, r_Te.at(layer, 1))
                            for h in range(4):
                                mm(work(6, h)[:, 0:SEQ], RKT[:, h, 0:P], RQT[:, h, :], start=True, stop=True)
                                ins = mm(work(6, h)[:, SEQ:384], RKT[:, h, P:SEQ], RQT[:, h, P:SEQ], start=True,
                                         stop=True)
                                if h % 2:
                                    ins.then_inc(r_s.sem, 1)
                        if at == (6, 8):
                            pe.wait_ge(r_sm.sem, r_sm.at(layer, 4))
                            for h in range(4):
                                c = slice(h * P, (h + 1) * P)
                                mm(work(6, 0)[:, c], SR[:, h, 0:P], RVv[:, 0, c], start=True, stop=True)
                                mm(work(6, 1)[:, c], SR[:, h, P:SEQ], RVv[:, 0, c], start=True, stop=False)
                                ins = mm(work(6, 1)[:, c], SR[:, h, SEQ:384], RVv[:, 1, c], start=False, stop=True)
                            ins.then_inc(r_o.sem, 1)
                        if at == (6, 13):
                            pe.wait_ge(r_rows.sem, r_rows.at(layer, 1))
                            rows_to_t2(RO, lambda b: work(6, 2 + b), 4)
                        if at == (7, 8):
                            pe.wait_ge(set_free.sem, set_free.at(layer, 7))
                            pe.wait_ge(m_rows.sem, m_rows.at(layer, 1))
                            rows_to_t2(XS, lambda b: work(7, b), 8)
                        if at == (7, 12):
                            gate_broadcast(layer, 1, 7, range(16))
                        if p >= 7:
                            pe.wait_ge(t2_ready.sem, t2_ready.at(layer, kt + 1 if p == 7 else 16))
                            left, lk = (T2h, T2l), OUT_ORDER[kt]
                        else:
                            left, lk = (HTh, HTl), kt
                        unit(layer, n, n, p, lk, left, kind, kt == 0, kt == KT - 1)
                        if ada_due(n, 24, 6) is not None:
                            half = ada_due(n, 24, 6)
                            b_ = ada_bank(p)
                            if p == 1:
                                pe.wait_ge(set_free.sem, set_free.at(layer, 1))
                            if p == 4:
                                pe.wait_ge(dt_abs.sem, dt_abs.at(layer, 1))
                            if p == 5:
                                pe.wait_ge(m_arg.sem, m_arg.at(layer, 8))
                            if p == 7:
                                pe.wait_ge(set_free.sem, set_free.at(layer, 7))
                            if p == 8:
                                pe.wait_ge(gated.sem, gated.at(layer, 4))
                            ada_sums(ada_mac.at(layer, 16 * (half + 1)), work(p, b_))
                        if 0 < n < FF0 * KT - 1 and ada_due(n - 1, 24, 6) is not None:
                            pe.wait_ge(ada_cols.sem, ada_cols.at(layer, ada_due(n - 1, 24, 6) + 1))
                with pe.Fori(0, GROUPS) as g:
                    for m in range(4 * KT):
                        s, kt = divmod(m, KT)
                        p = FF0 + s
                        if kt == 0:
                            if s == 0:
                                pe.wait_ge(ada_cols.sem, ada_cols.at(layer, 6))
                            if s < 2:
                                pe.wait_ge(gated.sem, gated.at(layer, g * 8 + 4 + 4 * s))
                            else:
                                pe.wait_ge(ff_relu.sem, ff_relu.at(layer, g * 8 + 4 * (s - 1)))
                            if s == 1:
                                pe.wait_ge(hT_hi.sem, hT_hi.at(layer, 32))
                        if s == 0 and kt in (0, 2, 6, 10):
                            with pe.If(g < 1):
                                x_transpose(layer, 1, (kt + 2) // 4)
                        if s == 0:
                            pe.wait_ge(hT_ready.sem, hT_ready.at(layer, 16 + kt + 1))
                        if s == 2 and kt % 2 == 0:
                            pe.wait_ge(ff_ready.sem, ff_ready.at(layer, g * 8 + kt // 2 + 1))
                        if m == 35:
                            with pe.If(g < 1):
                                pe.wait_ge(ff_relu.sem, ff_relu.at(layer, 8))
                                gate_broadcast(layer, 2, p, range(8))
                        left = (HTh, HTl) if s < 2 else (T2h, T2l)
                        unit(layer, g * 64 + FF0 * KT + m, m, p, kt, left, "cols" if s < 2 else "rows",
                             kt == 0, kt == KT - 1)
                        if ada_due(m, 32, 2) is not None:
                            half = ada_due(m, 32, 2)
                            with pe.If(g + 2 * layer < 3):
                                if s == 1:
                                    pe.wait_ge(ff_relu.sem, ff_relu.at(layer, g * 8 + 4))
                                else:
                                    pe.wait_ge(gated.sem, gated.at(layer, g * 8 + 12))
                                ada_sums(ada_mac.at(layer, g * 32 + 96 + 16 * (half + 1)), work(p, 3))
                                pe.wait_ge(ada_cols.sem, ada_cols.at(layer, g * 2 + 7 + half))
                        if m == 63:
                            with pe.If(g < 1):
                                gate_broadcast(layer, 3, p, range(8, 16))
                                pe.wait_ge(g_ready.sem, g_ready.at(layer, 3))


_INS = ["x", "c", "positions", "lb_logits", "w_in", "w_out", "w_ada", "b_ada", "ln_g", "ln_b", "hg_norm_w",
        "m_conv_w", "m_conv_b", "m_dt_bias", "m_a_log", "m_d", "m_norm_w", "w1", "w2"]


def kernel(**inputs):
    import concourse.bacc as _bacc
    from concourse.bass_utils import run_bass_kernel_spmd as _run

    nc = _bacc.Bacc("TRN2", target_bir_lowering=False, num_devices=1)
    nc.disable_value_cache = True
    arrays, args = {}, []
    for name in _INS + ["consts"]:
        a = constants() if name == "consts" else np.ascontiguousarray(inputs[name])
        arrays[f"in_{name}"] = a
        args.append(nc.dram_tensor(f"in_{name}", a.shape, mybir.dt.from_np(a.dtype), kind="ExternalInput").ap())
    args.append(nc.dram_tensor("out_0", (1, SEQ, D), F32, kind="ExternalOutput").ap())
    hybrid_trunk(nc, *args)
    r = _run(nc, [arrays], core_ids=[0])
    return r.results[0]["out_0"]
```

```python
import math
from contextlib import ExitStack

import numpy as np

import concourse.bass as bass
from concourse import mybir

ALU = mybir.AluOpType
ACT = mybir.ActivationFunctionType
AX = mybir.AxisListType
F32 = mybir.dt.float32
F32R = mybir.dt.float32r
BF16 = mybir.dt.bfloat16
I32 = mybir.dt.int32
ds = bass.ds

P = 128
D = 2048
SEQ = 256
DEPTH = 2
KT = D // P
DFF = 4 * D
IN_COLS = 6672
UW = 1024
RAW_SLOTS, W_SLOTS = 8, 4
PRO_SLOTS = 16
AHEAD = 2
ADA_LAG = 4
NPASS = 25
NUNIT = NPASS * KT
FF0 = 9
POOL_END = FF0 * KT - RAW_SLOTS
BY_POOL = [n for n in range(7, POOL_END) if n % 4 == 3 or (n % 4 == 1 and n // KT in (2, 3, 4, 7))]
POOL_UNITS = len(BY_POOL)
GROUPS = 4
ALPHA = (2 * DEPTH) ** 0.25
LN_EPS, RMS_EPS = 1e-5, 1e-6
COL0 = [2048, 3072, 5120, 6144, 0, 1024, 4096]
OUT_ORDER = [4, 5, 6, 7, 0, 1, 2, 3] + list(range(8, 16))
TWO_PI = 2 * math.pi
C1 = 6.28125
C2 = 0.001934814453125
C3 = TWO_PI - C1 - C2
MAGIC = 1.5 * 2.0 ** 23

K_ID, K_ML, K_TRI, K_DG = 0, 128, 128 + 9 * 128, 128 + 9 * 128 + 384
K_KEEP = K_DG + 1024
K_LM, K_FREQ = K_KEEP, K_KEEP + 1024
K_ALL = K_FREQ + 64
T_C, T_HGW, T_CB, T_MNW, T_CW, T_LB = 192, 208, 216, 240, 256, 352

LINKS = {"act": 0, "dve": 65, "pool": 7}


def constants():
    t = np.arange(P)[:, None]
    r = np.arange(P)[None, :]
    k = np.zeros((P, K_ALL), np.float32)
    k[:, K_ID:K_ID + P] = np.eye(P)
    for lv in range(7):
        s = 64 >> lv
        mid = (r // (2 * s)) * 2 * s + s
        k[:, K_ML + lv * P:K_ML + lv * P + P] = np.where(r >= mid, (t >= mid) & (t <= r), (t > r) & (t < mid))
        same = (t // (2 * s)) == (r // (2 * s))
        k[:, K_LM + lv * P:K_LM + lv * P + P] = same & (t % (2 * s) < s) & (r % (2 * s) >= s)
    k[:, K_ML + 7 * P:K_ML + 8 * P] = t > r
    k[:, K_ML + 8 * P:K_ML + 9 * P] = t <= r
    k[:, K_LM + 7 * P:K_LM + 8 * P] = np.eye(P)
    k[:, K_TRI:K_TRI + P] = t <= r
    k[:, K_TRI + P:K_TRI + 2 * P] = 1.0
    k[:, K_TRI + 2 * P:K_TRI + 3 * P] = t <= r
    i = np.arange(SEQ)[None, :]
    for h in range(4):
        lg = float(np.float32(math.log(1.0 - 2.0 ** (-5 - h))))
        k[:, K_DG + h * SEQ:K_DG + (h + 1) * SEQ] = np.where(i >= t, np.exp(lg * np.maximum(i - t, 0)), 0.0) * P ** -0.5
    expo = np.linspace(0.0, 1.0, 64, dtype=np.float32)
    k[:, K_FREQ:K_FREQ + 64] = np.float32(1.0) / (np.float32(10000.0) ** expo)
    return k


def hybrid_trunk(nc, x, c, positions, lb_logits, w_in, w_out, w_ada, b_ada, ln_g, ln_b, hg_norm_w,
                 m_conv_w, m_conv_b, m_dt_bias, m_a_log, m_d, m_norm_w, w1, w2, consts, out):
    with ExitStack() as ctx:
        place = {"at": (nc.sbuf_base + 63) // 64 * 64}

        def sb(name, shape, dt=F32, at=None):
            size = int(np.prod(shape[1:])) * (2 if dt == BF16 else 4)
            if at is None:
                at = place["at"]
                place["at"] += (size + 31) // 32 * 32
            t = nc.alloc_sbuf_tensor_at(name, shape, dt, offset=at)
            return t

        base = place["at"]
        X = sb("X", [P, 2, D])
        HTh = sb("HTh", [P, KT, SEQ], F32R)
        HTl = sb("HTl", [P, KT, SEQ], F32R)
        t2h_at = place["at"]
        T2h = sb("T2h", [P, KT, SEQ], F32R)
        t2l_at = place["at"]
        T2l = sb("T2l", [P, KT, SEQ], F32R)
        RAW = sb("RAW", [P, RAW_SLOTS, UW])
        WH = sb("WH", [P, W_SLOTS, UW], F32R)
        WL = sb("WL", [P, W_SLOTS, UW], F32R)
        ADR = sb("ADR", [P, 2, UW])
        ACC = sb("ACC", [P, UW])
        K = sb("K", [P, K_KEEP])
        LM = sb("LM", [P, 8 * P], BF16)
        COS = sb("COS", [P, 2, 64])
        SIN = sb("SIN", [P, 2, 64])
        PT = sb("PT", [P, 360])
        ADA = sb("ADA", [P, DEPTH * 96])
        CT = sb("CT", [P, KT])
        LBT = sb("LBT", [P, DEPTH * 4])
        OML = sb("OML", [P, DEPTH * 4])
        MD = sb("MD", [P, DEPTH * 16])
        DTB = sb("DTB", [16, DEPTH])
        NA = sb("NA", [16, DEPTH])
        SC = sb("SC", [P, 2, KT])
        SH = sb("SH", [P, 2, KT])
        GC = sb("GC", [P, KT])
        GCh = sb("GCh", [P, KT], F32R)
        GCl = sb("GCl", [P, KT], F32R)
        IDR = sb("IDR", [P, P], F32R)
        cLB = sb("cLB", [P, 4])
        cOML = sb("cOML", [P, 4])
        cHGW = sb("cHGW", [P, 4])
        cCB = sb("cCB", [P, 12])
        cCW = sb("cCW", [P, 4, 12])
        cMNW = sb("cMNW", [P, 8])
        cMD = sb("cMD", [P, 16])
        cDTB = sb("cDTB", [16, 1])
        cNA = sb("cNA", [16, 1])
        BN = sb("BN", [P, 2, 4, 6])
        MV = sb("MV", [P, 2, 2])
        NMR = sb("NMR", [P, 2])
        RV = sb("RV", [P, 8])
        RR = sb("RR", [P, 8])
        RA = sb("RA", [P, 8])
        SSQ = sb("SSQ", [P, 8])
        DTC = sb("DTC", [P, 2, 2, 16])
        CROSSK = sb("CROSSK", [P, P])
        AL1 = sb("AL1", [P, 1])
        IDLE = sb("IDLE", [P, 4])
        ACT_IDLE = sb("ACT_IDLE", [P, 1])
        SM = sb("SM", [P, P])
        SX = sb("SX", [P, P])

        w_at = place["at"]
        KB = 1024

        def W(name, kb, shape, dt=F32):
            return sb(name, shape, dt, at=w_at + kb * KB)

        XS = W("XS", 0, [P, 2, 1024])
        QT = W("QT", 8, [P, 4, SEQ])
        KTt = W("KTt", 12, [P, 4, SEQ])
        LF = W("LF", 16, [P, 2, 512])
        V = W("V", 20, [P, 2, 512])
        SG = W("SG", 24, [P, 2, 512])
        MS = W("MS", 28, [P, 8, P])
        place["at"] += 32 * KB
        assert place["at"] <= nc.sbuf_usable_end, (place["at"], nc.sbuf_usable_end)
        E2 = sb("E2", [P, 2, 8, P], at=t2h_at)
        EQ2 = sb("EQ2", [P, 2, 8, P], at=t2l_at)
        E, EQ = E2[:, 0], EQ2[:, 0]
        U = sb("U", [P, 8, SEQ], at=t2h_at + 8 * KB)
        CV = sb("CV", [P, 8, SEQ], at=t2l_at + 8 * KB)
        XD = sb("XD", [P, 2, 1024], at=t2h_at + 8 * KB)
        BU = W("BU", 4, [P, 4, SEQ])
        DTR = W("DTR", 1, [16, SEQ])
        BC = W("BC", 8, [P, 4, SEQ])
        CB2 = W("CB2", 12, [P, 4, SEQ])
        SB = W("SB", 12, [P, 2, 384])
        DTW = [sb(f"DTW{i}", [16, SEQ], at=w_at + (28 + i) * KB) for i in range(4)]
        CUM = sb("CUM", [16, SEQ], at=t2l_at + 14 * KB)
        DTT = sb("DTT", [16, SEQ], at=t2l_at + 15 * KB)
        MW = sb("MW", [P, 2, 2, 384], at=t2l_at + 8 * KB)
        QK = W("QK", 20, [P, 2, 1024])
        RA1 = W("RA1", 16, [P, 1024])
        RB1 = W("RB1", 28, [P, 1024])
        RVv = W("RVv", 8, [P, 2, 512])
        RSG = W("RSG", 12, [P, 2, 512])
        RQT = sb("RQT", [P, 4, SEQ], at=t2h_at + 8 * KB)
        RKT = sb("RKT", [P, 4, SEQ], at=t2h_at + 12 * KB)
        SR = sb("SR", [P, 4, 384], at=t2l_at + 8 * KB)
        RO = W("RO", 28, [P, 2, 512])
        ZS = W("ZS", 20, [P, 2, 1024])
        JUNK = W("JUNK", 16, [P, 8, P])
        TX = W("TX", 0, [P, 4, SEQ])
        TM = {1: W("TM1", 20, [P, 4, SEQ]), 2: W("TM2", 8, [P, 4, SEQ])}
        TM[3] = TM[2]
        HJ = W("HJ", 0, [P, P])
        GB = W("GB", 8, [P, D])
        LNG = W("LNG", 16, [P, D])
        LNB = W("LNB", 24, [P, D])
        R = W("R", 0, [P, 2, 512])
        SQ = W("SQ", 4, [P, 2, 512])
        Y4 = W("Y4", 0, [P, 4, 512])
        PACC = [[ACC, W("ACC2", 24, [P, UW])], [W("ACC3", 28, [P, UW]), W("ACC4", 4, [P, UW])]]
        RAW2 = sb("RAW2", [P, PRO_SLOTS - RAW_SLOTS, UW], at=t2h_at)
        ST = W("ST", 0, [P, 3, P])
        LMs = W("LMs", 8, [P, 1024])
        FREQ = W("FREQ", 12, [P, 64])
        POSI = sb("POSI", [P, 2], I32, at=w_at + 13 * KB)
        POSF = W("POSF", 14, [P, 2])
        ANG = W("ANG", 16, [P, 2, 64])
        RND = W("RND", 17, [P, 2, 64])
        S2 = W("S2", 18, [P, 2, 64])
        E16 = W("E16", 19, [P, KT])
        LX = W("LX", 20, [P, 8])
        LMX = W("LMX", 21, [P, 4])
        AL = W("AL", 22, [16, DEPTH])

        PB = [ctx.enter_context(nc.psum_tensor(f"PB{i}", [P, 512], F32)) for i in range(8)]

        class Signal:

            def __init__(self, name, per=0, first=0):
                self.sem = ctx.enter_context(nc.semaphore(name))
                self.per, self.first = per, first

            def at(self, layer, count):
                return self.first + layer * self.per + count

        raw_in = [Signal(f"raw_in{i}", 16 * NUNIT // RAW_SLOTS, 16 * 64 // PRO_SLOTS) for i in range(RAW_SLOTS)]
        raw2_in = [Signal(f"raw2_in{i}") for i in range(PRO_SLOTS - RAW_SLOTS)]
        hi_done = Signal("hi_done", NUNIT)
        lo_done = Signal("lo_done", NUNIT - POOL_UNITS, RAW_SLOTS)
        lo_pool = Signal("lo_pool", POOL_UNITS)
        unit_done = Signal("unit_done", NUNIT, W_SLOTS)
        set_free = Signal("set_free", 7)
        ada_in = [Signal(f"ada_in{i}", 16 * 96) for i in range(2)]
        ada_mac = Signal("ada_mac", 192, 64 + 2)
        ada_sum = Signal("ada_sum", 12, 4)
        ada_cols = Signal("ada_cols", 12, 4)
        x_last = Signal("x_last", 4)
        x_ready = Signal("x_ready", 8, 4)
        xT = Signal("xT", 16)
        hT_hi = Signal("hT_hi", 32)
        hT_ready = Signal("hT_ready", 32)
        cols_set = Signal("cols_set", 2)
        t2_T = Signal("t2_T", 3)
        t2_hi = Signal("t2_hi", 16)
        t2_ready = Signal("t2_ready", 16)
        rs_in = Signal("rs_in", 5)
        rs_act = Signal("rs_act", 5)
        rs_out = Signal("rs_out", 5)
        hg_f = Signal("hg_f", 4)
        hg_k = Signal("hg_k", 1)
        hg_lnf = Signal("hg_lnf", 1)
        hg_logT = Signal("hg_logT", 1)
        hg_log = Signal("hg_log", 1)
        hg_x = Signal("hg_x", 8)
        hg_e = Signal("hg_e", 8)
        hg_eq = Signal("hg_eq", 8)
        hg_ek = Signal("hg_ek", 8)
        hg_s = Signal("hg_s", 8)
        hg_ms = Signal("hg_ms", 8)
        hg_sm = Signal("hg_sm", 8)
        hg_sx = Signal("hg_sx", 4)
        hg_o = Signal("hg_o", 8)
        hg_oe = Signal("hg_oe", 8)
        hg_rows = Signal("hg_rows", 1)
        cv_in = Signal("cv_in", 12)
        cv_done = Signal("cv_done", 2)
        cv_act = Signal("cv_act", 2)
        dt_abs = Signal("dt_abs", 1)
        dt_exp = Signal("dt_exp", 1)
        dt_u = Signal("dt_u", 1)
        dt_ln = Signal("dt_ln", 1)
        dt_cum = Signal("dt_cum", 1)
        dt_rows = Signal("dt_rows", 1)
        dt_ready = Signal("dt_ready", 1)
        xs_T = Signal("xs_T", 2)
        xs_rows = Signal("xs_rows", 2)
        xd_ready = Signal("xd_ready", 1)
        xsd_ready = Signal("xsd_ready", 1)
        m_s = Signal("m_s", 2)
        m_sm = Signal("m_sm", 2)
        m_cum = Signal("m_cum", 8)
        m_arg = Signal("m_arg", 8)
        m_exp = Signal("m_exp", 8)
        m_m = Signal("m_m", 8)
        m_y = Signal("m_y", 8)
        m_ye = Signal("m_ye", 2)
        m_z = Signal("m_z", 1)
        m_sq = Signal("m_sq", 1)
        m_rows = Signal("m_rows", 1)
        r_rot = Signal("r_rot", 1)
        r_T = Signal("r_T", 1)
        r_Te = Signal("r_Te", 1)
        r_s = Signal("r_s", 2)
        r_sm = Signal("r_sm", 4)
        r_o = Signal("r_o", 1)
        r_oe = Signal("r_oe", 1)
        r_rows = Signal("r_rows", 1)
        g_cols = Signal("g_cols", 3)
        g_bc = Signal("g_bc", 3)
        g_ready = Signal("g_ready", 3)
        gated = Signal("gated", 40)
        x_add = Signal("x_add", 40)
        ln_gb_in = Signal("ln_gb_in", 64)
        ln_norm = Signal("ln_norm", 6)
        ln_mul = Signal("ln_mul", 6)
        ff_relu = Signal("ff_relu", 32)
        ff_sq = Signal("ff_sq", 32)
        ff_hi = Signal("ff_hi", 32)
        ff_ready = Signal("ff_ready", 32)
        pro_st = Signal("pro_st")
        pro_in = Signal("pro_in")
        pro_x = Signal("pro_x")
        pro_T = Signal("pro_T")
        pro_pt = Signal("pro_pt")
        pro_act = Signal("pro_act")
        pro_dve = Signal("pro_dve")
        out_done = Signal("out_done")
        order = {e: Signal(f"{e}_order", LINKS[e]) for e in LINKS}

        class Order:

            def __init__(self, eng, sig):
                self.eng, self.sig, self.layer, self.n = eng, sig, None, 0

            def start(self, layer):
                if self.layer is None:
                    self.sig.first = self.n
                self.layer, self.n = layer, 0

            def __call__(self, ins):
                ins.then_inc(self.sig.sem, 1)
                self.n += 1
                self.eng.wait_ge(self.sig.sem, self.n if self.layer is None else self.sig.at(self.layer, self.n))

            def end(self, name):
                assert self.n == LINKS[name], (name, self.n)

        w_in_r = w_in.rearrange("l k n -> (l k) n")
        w_out_r = w_out.rearrange("l k n -> (l k) n")
        w_ada_r = w_ada.rearrange("l k n -> (l k) n")
        w1_r = w1.rearrange("l k n -> (l k) n")
        w2_r = w2.rearrange("l k n -> (l k) n")
        ln_g_r = ln_g.rearrange("l s n -> (l s) n")
        ln_b_r = ln_b.rearrange("l s n -> (l s) n")
        x_r = x.rearrange("b (r p) n -> p (b r) n", p=P)
        out_r = out.rearrange("b (r p) n -> p (b r) n", p=P)
        ident = K[:, K_ID:K_ID + P]
        ones = K[:, K_TRI + P:K_TRI + P + 1]

        HG_X, HG_X1, HG_S, HG_M = [2, 5, 8, 11], [3, 6, 9, 12], [6, 9, 12, 15], [7, 10, 13, 15]
        HG_O = [(2, 8), (2, 11), (2, 14), (3, 4), (3, 8), (3, 11), (3, 14), (4, 4)]
        CONV = [(3, 4), (3, 5), (3, 7), (3, 8), (3, 10), (3, 11), (3, 13), (3, 14)]
        HG_EARLY = (1, 5)
        M_CUM, M_ARG = [3, 4, 5, 6, 7, 8, 10, 11], [4, 5, 6, 7, 8, 9, 11, 12]
        M_MUL, M_Y = [5, 6, 7, 8, 9, 10, 12, 13], [6, 7, 8, 9, 11, 12, 13, 14]

        def ada_bank(p):
            return 1 if p < 4 else 3

        def width(p):
            return 528 if p == 3 else UW

        def bank(p, b):
            return PB[4 * (p % 2) + b]

        def work(p, b):
            return PB[4 * (1 - p % 2) + b]

        def ada_units(n, span, total):
            half, m = divmod(n, span)
            live = span - ADA_LAG
            if half >= total or m >= live:
                return []
            return [half * 16 + k for k in range(m * 16 // live, (m + 1) * 16 // live)]

        def ada_due(n, span, total):
            half, m = divmod(n, span)
            return half if half < total and m == span - ADA_LAG else None

        def pro_slot(a):
            i = a % PRO_SLOTS
            return (RAW[:, i, :], raw_in[i].sem) if i < RAW_SLOTS else (RAW2[:, i - RAW_SLOTS, :],
                                                                        raw2_in[i - RAW_SLOTS].sem)

        def by_pool(n):
            return isinstance(n, int) and n in BY_POOL

        def lo_ready(layer, n):
            before = sum(u <= n for u in BY_POOL) if isinstance(n, int) else POOL_UNITS
            if by_pool(n):
                return lo_pool.sem, lo_pool.at(layer, before)
            return lo_done.sem, lo_done.at(layer, n + 1 - before)

        def bc(ap, shape):
            return ap.broadcast_to(shape)

        block = ctx.enter_context(nc.Block())

        @block.sync
        def _(sp):
            def ada_load(count, unit, row, col):
                sp.wait_ge(ada_mac.sem, count(unit + 1))
                sp.dma_start(ADR[:, unit % 2, :], w_ada_r[ds(row, P), ds(col, UW)]
                             ).then_inc(ada_in[unit % 2].sem, 16)

            def raw_load(layer, n, slot, src):
                if isinstance(n, int) and n < RAW_SLOTS:
                    sp.wait_ge(lo_done.sem, lo_done.at(layer, n + 1) - RAW_SLOTS)
                else:
                    sp.wait_ge(*lo_ready(layer, n - RAW_SLOTS))
                w = src.shape[1]
                sp.dma_start(RAW[:, slot, 0:w], src).then_inc(raw_in[slot].sem, 16)

            for a in range(64):
                if a >= PRO_SLOTS:
                    sp.wait_ge(ada_mac.sem, a - PRO_SLOTS + 3)
                dst, arrived = pro_slot(a)
                sp.dma_start(dst, w_ada_r[(a % 16) * P:(a % 16 + 1) * P, (a // 16) * UW:(a // 16 + 1) * UW]
                             ).then_inc(arrived, 16)
            with sp.Fori(0, DEPTH) as layer:
                for p in range(FF0):
                    for kt in range(KT):
                        n = p * KT + kt
                        if p < 7:
                            src = w_in_r[ds(layer * D + kt * P, P), COL0[p]:COL0[p] + width(p)]
                        else:
                            src = w_out_r[ds(layer * D + OUT_ORDER[kt] * P, P), (p - 7) * UW:(p - 6) * UW]
                        raw_load(layer, n, n % RAW_SLOTS, src)
                        for a in ada_units(n - ADA_LAG, 24, 6) if n >= ADA_LAG else ():
                            ada_load(lambda k: ada_mac.at(layer, k) - 2, a, layer * D + (a % 16) * P,
                                     (4 + a // 16) * UW)
                with sp.Fori(0, GROUPS) as g:
                    def group(ada):
                        for m in range(4 * KT):
                            s, kt = divmod(m, KT)
                            if s < 2:
                                src = w1_r[ds(layer * D + kt * P, P), ds(g * D + s * UW, UW)]
                            else:
                                src = w2_r[ds(layer * DFF + g * D + kt * P, P), (s - 2) * UW:(s - 1) * UW]
                            raw_load(layer, FF0 * KT + g * 64 + m, m % RAW_SLOTS, src)
                            for a in ada_units(m - ADA_LAG, 32, 2) if ada and m >= ADA_LAG else ():
                                q = layer * 12 + 10 + g * 2 + a // 16
                                ada_load(lambda k: ada_mac.at(layer, 96 + g * 32 + k) - 2, a,
                                         ((q // 12) % 2) * D + (a % 16) * P, (q % 12) * UW)
                    with sp.If(g + 2 * layer < 3):
                        group(True)
                    with sp.Else():
                        group(False)
            for ch in range(4):
                sp.wait_ge(x_ready.sem, x_ready.at(DEPTH - 1, 4 + ch + 1))
                cols = slice(ch * 512, (ch + 1) * 512)
                sp.dma_start(out_r[:, :, cols], X[:, :, cols]).then_inc(out_done.sem, 16)
            sp.wait_ge(out_done.sem, 16 * 4)

        @block.gpsimd
        def _(pool):
            link = Order(pool, order["pool"])
            pool.memset(RV[:, :], 1.0)
            pool.memset(RR[:, :], 1.0).then_inc(unit_done.sem, W_SLOTS)
            pool.memset(AL1[:, :], ALPHA)
            pool.memset(IDLE[:, :], 0.0)
            pool.memset(SSQ[:, :], 1.0).then_inc(ada_mac.sem, 2)
            pool.dma_start(X[:, :, :], x_r).then_inc(pro_x.sem, 16)
            pool.wait_ge(pro_x.sem, 16)
            pool.memset(NMR[:, :], 0.0).then_inc(x_ready.sem, 4)

            def scale_chunk(layer, s, ch):
                pool.wait_ge(xT.sem, xT.at(layer, 8 * s + 2 * ch + 2))
                xc = X[:, :, ch * 512:(ch + 1) * 512]
                ins = pool.tensor_tensor(xc, xc, bc(AL1[:, :].unsqueeze(1), [P, 2, 512]), ALU.mult)
                if ch == 3:
                    link(ins)

            def add_y(layer, k, half):
                for b in range(4):
                    r, col = b // 2, half * UW + (b % 2) * 512
                    pool.wait_ge(gated.sem, gated.at(layer, k + b + 1))
                    xc = X[:, r, col:col + 512]
                    pool.tensor_tensor(xc, xc, R[:, b % 2, :], ALU.add).then_inc(x_add.sem, 1)

            def last_add(layer, k):
                for c in range(2):
                    pool.wait_ge(gated.sem, gated.at(layer, k + c + 1))
                    xc = X[:, 1, UW + c * 512:UW + (c + 1) * 512]
                    pool.tensor_tensor(xc, xc, Y4[:, 2 + c, :], ALU.add).then_inc(x_last.sem, 1)

            def load_ln(layer, s):
                pool.dma_start(LNG[:, :], ln_g_r[ds(layer * 2 + s, 1), :].squeeze(0).partition_broadcast(P)
                               ).then_inc(ln_gb_in.sem, 16)
                pool.dma_start(LNB[:, :], ln_b_r[ds(layer * 2 + s, 1), :].squeeze(0).partition_broadcast(P)
                               ).then_inc(ln_gb_in.sem, 16)

            def ln_add(layer, s):
                for ch in range(1, 4):
                    if ch == 1:
                        pool.wait_ge(x_ready.sem, x_ready.at(layer, 4 * s + 1))
                    pool.wait_ge(ln_mul.sem, ln_mul.at(layer, 3 * s + ch))
                    xc = X[:, :, ch * 512:(ch + 1) * 512]
                    pool.tensor_tensor(xc, xc, bc(LNB[:, ch * 512:(ch + 1) * 512].unsqueeze(1), [P, 2, 512]),
                                       ALU.add).then_inc(x_ready.sem, 1)

            with pool.Fori(0, DEPTH) as layer:
                link.start(layer)
                for p in range(FF0):
                    for kt in range(KT):
                        at, n = (p, kt), p * KT + kt
                        if p == 0 and kt in (1, 3, 7, 11):
                            scale_chunk(layer, 0, (kt + 1) // 4)
                        if p in (2, 3) and kt in HG_X1:
                            i = (p - 2) * 4 + HG_X1.index(kt)
                            h, t = divmod(i, 2)
                            pool.wait_ge(hg_eq.sem, hg_eq.at(layer, i + 1))
                            if i == 0:
                                pool.wait_ge(hg_k.sem, hg_k.at(layer, 1))
                            kk = KTt[:, h, t * P:(t + 1) * P]
                            pool.tensor_tensor(E2[:, i % 2, 0:7, :], E2[:, i % 2, 0:7, :],
                                               bc(kk.unsqueeze(1), [P, 7, P]), ALU.mult).then_inc(hg_ek.sem, 1)
                        if p in (2, 3) and kt - 1 in HG_X1[0::2]:
                            i = (p - 2) * 4 + HG_X1.index(kt - 1)
                            if i >= 2:
                                pool.wait_ge(hg_s.sem, hg_s.at(layer, i))
                            pool.tensor_tensor(CROSSK[:, :], E2[:, i % 2, 7, :], KTt[:, i // 2, 0:P], ALU.mult)
                        if at == (4, 6):
                            pool.wait_ge(hg_oe.sem, hg_oe.at(layer, 8))
                            link(pool.tensor_tensor(LF[:, :, :], LF[:, :, :], SG[:, :, :], ALU.mult))
                            pool.wait_ge(rs_out.sem, rs_out.at(layer, 1))
                            lf8 = LF[:, :, :].rearrange("p t (h d) -> p (t h) d", d=P)
                            pool.tensor_tensor(lf8, lf8, bc(RR[:, 0:8].unsqueeze(2), [P, 8, P]), ALU.mult
                                               ).then_inc(hg_rows.sem, 1)
                        if at == (4, 13):
                            pool.wait_ge(dt_ready.sem, dt_ready.at(layer, 1))
                            pool.wait_ge(xs_rows.sem, xs_rows.at(layer, 2))
                            for r in range(2):
                                xs = XS[:, r, :].rearrange("p (h d) -> p h d", d=64)
                                xd = XD[:, r, :].rearrange("p (h d) -> p h d", d=64)
                                ins = pool.tensor_tensor(xd, xs, bc(DTC[:, r, 0, :].unsqueeze(2), [P, 16, 64]),
                                                         ALU.mult)
                            ins.then_inc(xd_ready.sem, 1)
                        if at == (5, 0):
                            for r in range(2):
                                xs = XS[:, r, :].rearrange("p (h d) -> p h d", d=64)
                                ins = pool.tensor_tensor(xs, xs, bc(cMD[:, :].unsqueeze(2), [P, 16, 64]), ALU.mult)
                            ins.then_inc(xsd_ready.sem, 1)
                        if at in ((5, 4), (5, 8)):
                            r = kt // 4 - 1
                            if r == 0:
                                pool.wait_ge(set_free.sem, set_free.at(layer, 5))
                            qk = QK[:, r, :].rearrange("p (h f) -> p h f", f=64)
                            a1 = RA1[:, :].rearrange("p (h f) -> p h f", f=64)
                            b1 = RB1[:, :].rearrange("p (h f) -> p h f", f=64)
                            pool.tensor_tensor(a1, qk, bc(COS[:, r, :].unsqueeze(1), [P, 16, 64]), ALU.mult)
                            link(pool.tensor_tensor(b1, qk, bc(SIN[:, r, :].unsqueeze(1), [P, 16, 64]), ALU.mult))
                            qh = QK[:, r, :].rearrange("p (h s f) -> p h s f", s=2, f=64)
                            ah = RA1[:, :].rearrange("p (h s f) -> p h s f", s=2, f=64)
                            bh = RB1[:, :].rearrange("p (h s f) -> p h s f", s=2, f=64)
                            pool.tensor_tensor(qh[:, :, 0, :], ah[:, :, 0, :], bh[:, :, 1, :], ALU.subtract)
                            ins = pool.tensor_tensor(qh[:, :, 1, :], bh[:, :, 0, :], ah[:, :, 1, :], ALU.add)
                            if r == 0:
                                link(ins)
                            else:
                                ins.then_inc(r_rot.sem, 1)
                        if at == (6, 10):
                            pool.wait_ge(r_oe.sem, r_oe.at(layer, 1))
                            link(pool.tensor_tensor(RO[:, :, :], RO[:, :, :], RSG[:, :, :], ALU.mult))
                            pool.wait_ge(rs_out.sem, rs_out.at(layer, 2))
                            ro8 = RO[:, :, :].rearrange("p t (h d) -> p (t h) d", d=P)
                            pool.tensor_tensor(ro8, ro8, bc(RR[:, 0:8].unsqueeze(2), [P, 8, P]), ALU.mult
                                               ).then_inc(r_rows.sem, 1)
                        if at == (7, 10):
                            pool.wait_ge(t2_T.sem, t2_T.at(layer, 3))
                            load_ln(layer, 0)
                        if at == (8, 2):
                            add_y(layer, 0, 0)
                        if by_pool(n + AHEAD):
                            m, w = n + AHEAD, width((n + AHEAD) // KT)
                            pool.wait_ge(hi_done.sem, hi_done.at(layer, m + 1))
                            pool.tensor_tensor(WL[:, m % W_SLOTS, 0:w], RAW[:, m % RAW_SLOTS, 0:w],
                                               WH[:, m % W_SLOTS, 0:w].bitcast(F32), ALU.subtract
                                               ).then_inc(lo_pool.sem, 1)
                last_add(layer, 4)
                ln_add(layer, 0)
                pool.wait_ge(x_ready.sem, x_ready.at(layer, 4))
                load_ln(layer, 1)
                for ch in range(4):
                    scale_chunk(layer, 1, ch)
                pool.tensor_tensor(IDLE[:, 1:2], IDLE[:, 0:1], IDLE[:, 0:1], ALU.mult)
                with pool.Fori(0, GROUPS) as g:
                    with pool.If(g > 0):
                        add_y(layer, 4 + g * 8, 1)
                    for i in range(8):
                        pool.wait_ge(ff_relu.sem, ff_relu.at(layer, g * 8 + i + 1))
                        if i >= 2:
                            pool.wait_ge(ff_ready.sem, ff_ready.at(layer, g * 8 + i - 1))
                        pool.tensor_tensor(SQ[:, i % 2, :], R[:, i % 2, :], R[:, i % 2, :], ALU.mult
                                           ).then_inc(ff_sq.sem, 1)
                    add_y(layer, 8 + g * 8, 0)
                last_add(layer, 36)
                ln_add(layer, 1)
                link.end("pool")

        @block.scalar
        def _(act):
            link = Order(act, order["act"])
            loads = [
                (K[:, P:], consts[:, P:K_KEEP]), (LMs[:, :], consts[:, K_LM:K_LM + 1024]),
                (FREQ[:, :], consts[:, K_FREQ:K_FREQ + 64]),
                (POSI[:, :], positions.rearrange("b (r p) -> p (b r)", p=P)),
                (DTB[:, :], m_dt_bias.rearrange("l h -> h l")), (AL[:, :], m_a_log.rearrange("l h -> h l")),
                (MD[:, :], m_d.rearrange("l h -> (l h)").partition_broadcast(P)),
            ]
            bt = b_ada.rearrange("l (t p) -> (l t) p", p=P)
            first = [(ST[:, 0, :], bt[0:128, :]), (ST[0:64, 1, :], bt[128:192, :]),
                      (ST[64:80, 1, :], c.rearrange("b (t p) -> (b t) p", p=P)),
                      (ST[80:88, 1, :], hg_norm_w.rearrange("l (t p) -> (l t) p", p=P)),
                      (ST[88:112, 1, :], m_conv_b.rearrange("l (t p) -> (l t) p", p=P)),
                      (ST[112:128, 1, :], m_norm_w.rearrange("l (t p) -> (l t) p", p=P)),
                      (ST[0:96, 2, :], m_conv_w.rearrange("l k (t p) -> (l k t) p", p=P)),
                      (ST[96:104, 2, :], lb_logits.rearrange("l (t p) -> (l t) p", p=P))]
            for dst, src in [(K[:, 0:P], consts[:, 0:P])] + first:
                act.dma_start(dst, src).then_inc(pro_st.sem, 16)
            for dst, src in loads:
                act.dma_start(dst, src, allow_slow_non_contiguous=True).then_inc(pro_in.sem, 16)
            act.wait_ge(pro_T.sem, 1)
            act.activation(PT[:, :], PB[0][:, 0:360], ACT.Copy).then_inc(pro_pt.sem, 1)
            act.wait_ge(pro_pt.sem, 1)
            act.activation(E16[:, :], PT[:, T_C:T_C + KT], ACT.Exp, scale=-1.0).then_inc(pro_act.sem, 1)
            act.wait_ge(pro_in.sem, 16 * 7)
            act.activation(AL[:, :], AL[:, :], ACT.Exp).then_inc(pro_act.sem, 1)
            act.wait_ge(pro_dve.sem, 1)
            act.activation(LX[:, :], LX[:, :], ACT.Exp).then_inc(pro_act.sem, 1)
            act.wait_ge(pro_dve.sem, 2)
            act.activation(SIN[:, :, :], ANG[:, :, :], ACT.Sin).then_inc(pro_act.sem, 1)
            act.activation(S2[:, :, :], ANG[:, :, :], ACT.Sin, scale=0.5).then_inc(pro_act.sem, 1)

            def hi_split(layer, n, m, loads_before, w=UW):
                act.wait_ge(raw_in[m % RAW_SLOTS].sem, raw_in[0].at(layer, (loads_before + 1) * 16))
                act.wait_ge(unit_done.sem, unit_done.at(layer, n + 1) - W_SLOTS)
                act.activation(WH[:, m % W_SLOTS, 0:w], RAW[:, m % RAW_SLOTS, 0:w], ACT.Copy
                               ).then_inc(hi_done.sem, 1)

            def t_out(tt_, src, k, dst, hi_sig, scale, bias):
                for j in range(2):
                    s = scale[:, j:j + 1] if scale is not None else 1.0
                    b = bias[:, j:j + 1] if bias is not None else 0.0
                    cols = src[:, j * SEQ:(j + 1) * SEQ]
                    act.activation(tt_[:, (k + j) % 4, :], cols, ACT.Identity, bias=b, scale=s)
                    act.activation(dst[:, j, :], cols, ACT.Identity, bias=b, scale=s).then_inc(hi_sig.sem, 1)

            def h_chunk(layer, s, ch):
                if ch == 0:
                    act.wait_ge(cols_set.sem, cols_set.at(layer, s + 1))
                for b in (2 * ch, 2 * ch + 1):
                    kt = 2 * b
                    if kt >= 4:
                        act.wait_ge(hT_ready.sem, hT_ready.at(layer, 16 * s + kt - 2))
                    act.wait_ge(xT.sem, xT.at(layer, 8 * s + b + 1))
                    t_out(TX, work(s * FF0, b % 4), kt, HTh[:, kt:kt + 2, :], hT_hi, SC[:, s, kt:kt + 2],
                          SH[:, s, kt:kt + 2])

            def t2_chunk(layer, which, p, banks, kt0, count0, weights=None):
                act.wait_ge(t2_T.sem, t2_T.at(layer, which))
                for i, b in enumerate(banks):
                    kt, k = kt0 + 2 * i, count0 + 2 * i
                    if k >= 6:
                        act.wait_ge(t2_ready.sem, t2_ready.at(layer, k - 2))
                    t_out(TM[which], work(p, b), k, T2h[:, kt:kt + 2, :], t2_hi,
                          None if weights is None else weights[:, 2 * i:2 * i + 2], None)

            def rsqrt(layer, k, cols):
                act.wait_ge(rs_in.sem, rs_in.at(layer, k))
                act.activation(RA[:, 0:cols], RV[:, 0:cols], ACT.Sqrt).then_inc(rs_act.sem, 1)

            def layer_norm_rows(layer, s, then=None):
                rsqrt(layer, 4 + s, 2)
                act.wait_ge(rs_out.sem, rs_out.at(layer, 4 + s))
                for ch in range(1, 4):
                    for r in range(2):
                        xc = X[:, r, ch * 512:(ch + 1) * 512]
                        ins = act.activation(xc, xc, ACT.Identity, bias=NMR[:, r:r + 1], scale=RR[:, r:r + 1])
                    ins.then_inc(ln_norm.sem, 1)
                    if ch == 1 and then:
                        then()

            def gate_rows(layer, k, p, parts):
                act.wait_ge(g_bc.sem, g_bc.at(layer, k))
                for i, b in enumerate(parts):
                    ins = act.activation(GB[:, b * 512:(b + 1) * 512], work(p, i)[:, :], ACT.Copy)
                ins.then_inc(g_ready.sem, 1)

            def evacuate(layer, p):
                act.wait_ge(unit_done.sem, unit_done.at(layer, KT * (p + 1)))
                halves = [(r, h) for r in range(2) for h in range(2)]
                if p == 0:
                    act.activation(QT[:, 0:2, :], bank(0, 0)[:, :], ACT.Copy)
                    act.activation(QT[:, 2:4, :], bank(0, 1)[:, :], ACT.Copy)
                    act.activation(EQ[:, 0:4, :], bank(0, 2)[:, :], ACT.Sigmoid)
                    ins = act.activation(EQ[:, 4:8, :], bank(0, 3)[:, :], ACT.Sigmoid)
                elif p in (1, 5):
                    val, gate = (V, SG) if p == 1 else (RVv, RSG)
                    for r in range(2):
                        act.activation(val[:, r, :], bank(p, 2 * r)[:, :], ACT.Copy)
                    for r in range(2):
                        ins = act.activation(gate[:, r, :], bank(p, 2 * r + 1)[:, :], ACT.Silu)
                elif p == 2:
                    for b in range(4):
                        ins = act.activation(U[:, 2 * b:2 * b + 2, :], bank(2, b)[:, :], ACT.Copy)
                elif p == 3:
                    act.activation(BU[:, 0:2, :], bank(3, 0)[:, :], ACT.Copy)
                    act.activation(BU[:, 2:4, :], bank(3, 1)[:, :], ACT.Copy)
                    ins = act.activation(DTR[:, :], bank(3, 2)[0:16, 0:SEQ], ACT.Copy)
                elif p == 4:
                    for r, h in halves:
                        ins = act.activation(QK[:, r, h * 512:(h + 1) * 512], bank(4, 2 * r + h)[:, :], ACT.Copy)
                else:
                    for r, h in halves:
                        ins = act.activation(ZS[:, r, h * 512:(h + 1) * 512], bank(6, 2 * r + h)[:, :], ACT.Silu)
                ins.then_inc(set_free.sem, 1)

            def conv_tap3(layer, p, src, dst, first, count):
                act.wait_ge(set_free.sem, set_free.at(layer, p + 1))
                for j in range(count):
                    t = first + j
                    act.activation(dst[:, j, :], src[:, j, :], ACT.Identity, bias=cCB[:, t:t + 1],
                                   scale=cCW[:, 3, t:t + 1]).then_inc(cv_in.sem, 1)

            def hg_out(layer, i, p):
                h, t = divmod(i, 2)
                act.wait_ge(hg_o.sem, hg_o.at(layer, i + 1))
                o = work(p, 2)[:, 0:P]
                act.activation(LF[:, t, h * P:(h + 1) * P], o, ACT.Copy)
                act.activation(HJ[:, :], o, ACT.Square, accum_out=SSQ[:, t * 4 + h:t * 4 + h + 1]
                               ).then_inc(hg_oe.sem, 1)

            for n in range(W_SLOTS):
                hi_split(0, n, n, 0)
            act.activation(ACT_IDLE[:, :], PT[:, 0:1], ACT.Identity)
            with act.Fori(0, DEPTH) as layer:
                link.start(layer)
                h_chunk(layer, 0, 0)
                for p in range(FF0):
                    for kt in range(KT):
                        n = p * KT + kt
                        if n + AHEAD >= W_SLOTS:
                            ahead = n + AHEAD
                            hi_split(layer, ahead, ahead, ahead // RAW_SLOTS, width(ahead // KT))
                        at = (p, kt)
                        if p == 0 and kt in (3, 7, 11):
                            h_chunk(layer, 0, (kt + 1) // 4)
                        if kt == 1 and 1 <= p <= 7:
                            evacuate(layer, p - 1)
                        if at == (1, 4):
                            act.wait_ge(hg_f.sem, hg_f.at(layer, 4))
                            act.activation(E[:, :, :], EQ[:, :, :], ACT.Ln).then_inc(hg_lnf.sem, 1)
                        if at == (1, 9):
                            act.wait_ge(hg_logT.sem, hg_logT.at(layer, 1))
                            act.activation(LF[:, 0, :], work(1, 0)[:, :], ACT.Copy)
                            act.activation(LF[:, 1, :], work(1, 1)[:, :], ACT.Copy).then_inc(hg_log.sem, 1)
                        if p in (2, 3) and kt in HG_X1:
                            i = (p - 2) * 4 + HG_X1.index(kt)
                            act.wait_ge(hg_x.sem, hg_x.at(layer, i + 1))
                            if i >= 2:
                                act.wait_ge(hg_s.sem, hg_s.at(layer, i - 1))
                            if i >= 2 and i % 2 == 0:
                                act.wait_ge(hg_ek.sem, hg_ek.at(layer, i))
                            act.activation(E2[:, i % 2, 0:4, :], work(p, 0)[:, :], ACT.Exp)
                            act.activation(E2[:, i % 2, 4:8, :], work(p, 1)[:, :], ACT.Exp).then_inc(hg_e.sem, 1)
                        if (p, kt - 1) in HG_O:
                            hg_out(layer, HG_O.index((p, kt - 1)), p)
                        if p in (2, 3) and kt in HG_M and HG_M.index(kt) % 2:
                            i = (p - 2) * 4 + HG_M.index(kt)
                            act.wait_ge(hg_s.sem, hg_s.at(layer, i + 1))
                            if i > 1:
                                act.wait_ge(hg_o.sem, hg_o.at(layer, i - 1))
                            act.activation(SX[:, :], work(p, 0)[:, 0:P], ACT.Copy).then_inc(hg_sx.sem, 1)
                        if at == (3, 3):
                            conv_tap3(layer, 2, U, CV, 0, 8)
                        if at == (4, 4):
                            act.wait_ge(cv_done.sem, cv_done.at(layer, 1))
                            act.activation(U[:, :, :], CV[:, :, :], ACT.Silu).then_inc(cv_act.sem, 1)
                        if at == (4, 3):
                            conv_tap3(layer, 3, BU, CB2, 8, 4)
                        if at == (4, 5):
                            act.wait_ge(dt_abs.sem, dt_abs.at(layer, 1))
                            act.activation(DTW[1][:, :], DTW[1][:, :], ACT.Exp, scale=-1.0).then_inc(dt_exp.sem, 1)
                        if at == (4, 6):
                            act.wait_ge(dt_u.sem, dt_u.at(layer, 1))
                            act.activation(DTW[3][:, :], DTW[2][:, :], ACT.Ln).then_inc(dt_ln.sem, 1)
                            rsqrt(layer, 1, 8)
                        if at == (4, 8):
                            act.wait_ge(cv_done.sem, cv_done.at(layer, 2))
                            act.activation(BC[:, :, :], CB2[:, :, :], ACT.Silu).then_inc(cv_act.sem, 1)
                        if at == (4, 9):
                            for r in range(2):
                                act.wait_ge(xs_T.sem, xs_T.at(layer, r + 1))
                                for b in range(2):
                                    ins = act.activation(XS[:, r, b * 512:(b + 1) * 512],
                                                         work(4, 2 * r + b)[:, :], ACT.Copy)
                                ins.then_inc(xs_rows.sem, 1)
                        if at == (4, 11):
                            t2_chunk(layer, 1, 4, (0, 1), 4, 0, cHGW)
                        if at == (4, 12):
                            act.wait_ge(dt_rows.sem, dt_rows.at(layer, 1))
                            act.activation(DTC[:, :, :, :], work(4, 2)[:, 0:64], ACT.Copy).then_inc(dt_ready.sem, 1)
                        if p == 5 and kt in M_ARG:
                            i = M_ARG.index(kt)
                            act.wait_ge(m_cum.sem, m_cum.at(layer, i + 1))
                            if i == 0:
                                act.wait_ge(dt_ready.sem, dt_ready.at(layer, 1))
                            if i >= 2:
                                act.wait_ge(m_y.sem, m_y.at(layer, i - 1))
                            for e in range(2):
                                hd = 2 * i + e
                                cb = work(5, 2 + i % 2)[:, e * SEQ:(e + 1) * SEQ]
                                act.activation(MW[:, i % 2, e, 0:SEQ], cb, ACT.Relu, scale=-1.0,
                                               bias=DTC[:, 0, 1, hd:hd + 1])
                                ins = act.activation(MW[:, i % 2, e, SEQ:384], cb[:, P:SEQ], ACT.Relu, scale=-1.0,
                                                     bias=DTC[:, 1, 1, hd:hd + 1])
                            ins.then_inc(m_arg.sem, 1)
                            act.wait_ge(m_arg.sem, m_arg.at(layer, i + 1))
                            act.activation(MW[:, i % 2, :, :], MW[:, i % 2, :, :], ACT.Exp, scale=-1.0
                                           ).then_inc(m_exp.sem, 1)
                        if at == (6, 4):
                            act.wait_ge(r_T.sem, r_T.at(layer, 1))
                            act.activation(RQT[:, 0:2, :], work(6, 0)[:, :], ACT.Copy)
                            act.activation(RQT[:, 2:4, :], work(6, 1)[:, :], ACT.Copy)
                            act.activation(RKT[:, 0:2, :], work(6, 2)[:, :], ACT.Copy)
                            act.activation(RKT[:, 2:4, :], work(6, 3)[:, :], ACT.Copy).then_inc(r_Te.sem, 1)
                        if at == (6, 9):
                            act.wait_ge(r_o.sem, r_o.at(layer, 1))
                            for t in range(2):
                                act.activation(RO[:, t, :], work(6, t)[:, :], ACT.Copy)
                                for h in range(4):
                                    ins = act.activation(JUNK[:, 4 * t + h, :], work(6, t)[:, h * P:(h + 1) * P], ACT.Square,
                                                         accum_out=SSQ[:, t * 4 + h:t * 4 + h + 1])
                            ins.then_inc(r_oe.sem, 1)
                            rsqrt(layer, 2, 8)
                        if at == (6, 14):
                            t2_chunk(layer, 2, 6, (2, 3), 0, 4)
                        if at == (7, 3):
                            act.wait_ge(m_z.sem, m_z.at(layer, 1))
                            for b in range(4):
                                ins = act.activation(ZS[:, b // 2, (b % 2) * 512:(b % 2 + 1) * 512], XS[:, b // 2, (b % 2) * 512:(b % 2 + 1) * 512],
                                                     ACT.Square, accum_out=SSQ[:, b:b + 1])
                            ins.then_inc(m_sq.sem, 1)
                            rsqrt(layer, 3, 4)
                        if at == (7, 9):
                            t2_chunk(layer, 3, 7, (0, 1, 2, 3), 8, 8, cMNW)
                        if at == (7, 13):
                            act.wait_ge(t2_ready.sem, t2_ready.at(layer, 16))
                            gate_rows(layer, 1, 7, range(4))
                for n in range(FF0 * KT + AHEAD, FF0 * KT + W_SLOTS):
                    hi_split(layer, n, n, n // RAW_SLOTS)
                layer_norm_rows(layer, 0, lambda: h_chunk(layer, 1, 0))
                with act.Fori(0, GROUPS) as g:
                    def relu_evac(s):
                        act.wait_ge(unit_done.sem, unit_done.at(layer, KT * (FF0 + g * 4 + s + 1)))
                        k0 = g * 8 + 4 * s
                        if s == 0:
                            act.wait_ge(x_add.sem, x_add.at(layer, 8 + g * 8))
                        for b in range(5):
                            if b < 4:
                                if b >= 2 or s == 1:
                                    act.wait_ge(ff_sq.sem, ff_sq.at(layer, k0 + b - 1))
                                act.activation(R[:, b % 2, :], bank(FF0 + s, b)[:, :], ACT.Relu
                                               ).then_inc(ff_relu.sem, 1)
                            if b >= 1:
                                act.wait_ge(ff_sq.sem, ff_sq.at(layer, k0 + b))
                                kt = 8 * s + 2 * (b - 1)
                                act.activation(T2h[:, kt:kt + 2, :], SQ[:, (b - 1) % 2, :], ACT.Copy
                                               ).then_inc(ff_hi.sem, 1)

                    def split(m):
                        hi_split(layer, g * 64 + FF0 * KT + m, m, g * 8 + FF0 * KT // RAW_SLOTS + m // RAW_SLOTS)

                    for m in range(4 * KT):
                        s, kt = divmod(m, KT)
                        if W_SLOTS <= m + AHEAD < 4 * KT:
                            split(m + AHEAD)
                        if s == 0 and kt in (3, 7, 11):
                            with act.If(g < 1):
                                h_chunk(layer, 1, (kt + 1) // 4)
                        if kt == 1 and s in (1, 2):
                            relu_evac(s - 1)
                        if m == 36:
                            with act.If(g < 1):
                                gate_rows(layer, 2, FF0 + s, (0, 1))
                    with act.If(g + GROUPS * layer < GROUPS * DEPTH - 1):
                        for m in range(4 * KT, 4 * KT + W_SLOTS):
                            split(m)
                    with act.If(g < 1):
                        gate_rows(layer, 3, FF0 + 3, (2, 3))
                layer_norm_rows(layer, 1)
                link.end("act")

        @block.vector
        def _(dve):
            link = Order(dve, order["dve"])
            tt, ts, stt = dve.tensor_tensor, dve.tensor_scalar, dve.scalar_tensor_tensor

            def ada_mul(in_sem, in_count, mac_count, sums, w, k):
                dve.wait_ge(in_sem, in_count)
                if k == 0:
                    if sums is not None:
                        dve.wait_ge(ada_sum.sem, sums)
                    ins = ts(ACC[:, :], w, CT[:, 0:1], None, ALU.mult)
                else:
                    dve.wait_ge(ada_mac.sem, mac_count)
                    ins = stt(ACC[:, :], w, CT[:, k:k + 1], ACC[:, :], ALU.mult, ALU.add)
                ins.then_inc(ada_mac.sem, 1)

            def ada_out(sum_count, col, bank_ap):
                dve.wait_ge(ada_sum.sem, sum_count)
                tt(ADA[:, ds(col, 8)], bank_ap[:, 0:8], PT[:, ds(col, 8)], ALU.add).then_inc(ada_cols.sem, 1)

            def tables():
                dve.wait_ge(pro_in.sem, 16 * 7)
                dve.wait_ge(pro_st.sem, 16 * 9)
                dve.tensor_copy(IDR[:, :], K[:, 0:P])
                dve.tensor_copy(LM[:, :], LMs[:, :])
                link(dve.tensor_copy(POSF[:, :], POSI[:, :]))
                for r in range(2):
                    ins = ts(ANG[:, r, :], FREQ[:, :], POSF[:, r:r + 1], None, ALU.mult)
                dve.wait_ge(pro_pt.sem, 1)
                lb0, lb1 = PT[:, T_LB:T_LB + 4], PT[:, T_LB + 4:T_LB + 8]
                link(tt(LMX[:, :], lb0, lb1, ALU.max))
                tt(LX[:, 0:4], lb0, LMX[:, :], ALU.subtract)
                tt(LX[:, 4:8], lb1, LMX[:, :], ALU.subtract).then_inc(pro_dve.sem, 1)
                link(ts(RND[:, :, :], ANG[:, :, :], 1.0 / TWO_PI, MAGIC, ALU.mult, ALU.add))
                link(ts(RND[:, :, :], RND[:, :, :], MAGIC, None, ALU.subtract))
                for part in (C1, C2, C3):
                    link(stt(ANG[:, :, :], RND[:, :, :], -part, ANG[:, :, :], ALU.mult, ALU.add))
                ts(ANG[:, :, :], ANG[:, :, :], 3.1415925, -3.1415925, ALU.min, ALU.max).then_inc(pro_dve.sem, 1)

            def tables_end():
                dve.wait_ge(pro_act.sem, 5)
                ts(NA[:, :], AL[:, :], -1.0, None, ALU.mult)
                link(tt(LMX[:, :], LX[:, 0:4], LX[:, 4:8], ALU.add))
                link(dve.reciprocal(LMX[:, :], LMX[:, :]))
                dve.memset(LBT[:, 0:4], 0.0)
                link(tt(LBT[:, 4:8], LX[:, 4:8], LMX[:, :], ALU.mult))
                ts(OML[:, :], LBT[:, :], -1.0, 1.0, ALU.mult, ALU.add)
                link(tt(S2[:, :, :], S2[:, :, :], S2[:, :, :], ALU.mult))
                link(ts(COS[:, :, :], S2[:, :, :], -2.0, 1.0, ALU.mult, ALU.add))

            dve.wait_ge(pro_act.sem, 1)
            link(ts(E16[:, :], E16[:, :], 1.0, None, ALU.add))
            link(dve.reciprocal(E16[:, :], E16[:, :]))
            link(tt(CT[:, :], E16[:, :], PT[:, T_C:T_C + KT], ALU.mult))
            for a in range(64):
                if a == 32:
                    tables()
                if a == 40:
                    tables_end()
                block_, arrived = pro_slot(a)
                acc, k = PACC[a // 16 % 2][a % 2], a % 16
                dve.wait_ge(arrived, 16 * (a // PRO_SLOTS + 1))
                if k < 2:
                    if a >= 32:
                        dve.wait_ge(ada_sum.sem, a // 16 - 1)
                    ins = ts(acc[:, :], block_, CT[:, k:k + 1], None, ALU.mult)
                else:
                    dve.wait_ge(ada_mac.sem, a + 1)
                    ins = stt(acc[:, :], block_, CT[:, k:k + 1], acc[:, :], ALU.mult, ALU.add)
                ins.then_inc(ada_mac.sem, 1)
                if 64 - PRO_SLOTS <= a < 64 - RAW_SLOTS:
                    dve.wait_ge(ada_mac.sem, a + 3)
                    dve.memset(IDLE[:, 3:4], 0.0).then_inc(lo_done.sem, 1)
                if a >= 16 and a % 16 == 8:
                    ada_out(a // 16, (a // 16 - 1) * 8, PB[4])
            dve.wait_ge(ada_mac.sem, 64 + 2)
            tt(PACC[1][0][:, :], PACC[1][0][:, :], PACC[1][1][:, :], ALU.add).then_inc(pro_dve.sem, 1)

            def lo_split(layer, n, m, w=UW):
                dve.wait_ge(hi_done.sem, hi_done.at(layer, n + 1))
                tt(WL[:, m % W_SLOTS, 0:w], RAW[:, m % RAW_SLOTS, 0:w], WH[:, m % W_SLOTS, 0:w].bitcast(F32),
                   ALU.subtract).then_inc(lo_done.sem, 1)

            def t_lo(tt_, hi_sig, hi_count, k, hi, lo, ready):
                dve.wait_ge(hi_sig.sem, hi_count)
                tt(lo, tt_[:, k % 4, :], hi.bitcast(F32), ALU.subtract).then_inc(ready.sem, 1)

            def h_chunk(layer, s, ch):
                for kt in range(4 * ch, 4 * ch + 4):
                    t_lo(TX, hT_hi, hT_hi.at(layer, 16 * s + kt + 1), kt, HTh[:, kt, :], HTl[:, kt, :], hT_ready)

            def t2_chunk(layer, which, kt0, count0, n):
                for i in range(n):
                    t_lo(TM[which], t2_hi, t2_hi.at(layer, count0 + i + 1), count0 + i, T2h[:, kt0 + i, :],
                         T2l[:, kt0 + i, :], t2_ready)

            def newton(layer, k, cols):
                dve.wait_ge(rs_act.sem, rs_act.at(layer, k))
                link(dve.reciprocal(RR[:, 0:cols], RA[:, 0:cols]))
                link(tt(RA[:, 0:cols], RR[:, 0:cols], RR[:, 0:cols], ALU.mult))
                link(tt(RA[:, 0:cols], RA[:, 0:cols], RV[:, 0:cols], ALU.mult))
                link(ts(RA[:, 0:cols], RA[:, 0:cols], -0.5, 1.5, ALU.mult, ALU.add))
                return tt(RR[:, 0:cols], RR[:, 0:cols], RA[:, 0:cols], ALU.mult)

            def rms(layer, k, cols, width_):
                ts(RV[:, 0:cols], SSQ[:, 0:cols], 1.0 / width_, RMS_EPS, ALU.mult, ALU.add).then_inc(rs_in.sem, 1)
                newton(layer, k, cols).then_inc(rs_out.sem, 1)

            def row_stats(layer, chunks, adds, last=None):
                dve.wait_ge(x_add.sem, adds)
                for r in range(2):
                    if last is not None and r:
                        dve.wait_ge(x_last.sem, x_last.at(layer, last))
                    for ch in chunks:
                        ins = dve.bn_stats(BN[:, r, ch, :], X[:, r, ch * 512:(ch + 1) * 512])
                return ins

            def layer_norm_rows(layer, s, stats, units=(), then=None):
                link(stats)
                dve.memset(IDLE[:, 2:3], 0.0)
                dve.bn_aggr(MV[:, 0, :], BN[:, 0, :, :].rearrange("p a b -> p (a b)"))
                link(dve.bn_aggr(MV[:, 1, :], BN[:, 1, :, :].rearrange("p a b -> p (a b)")))
                ts(RV[:, 0:2], MV[:, :, 1], LN_EPS, None, ALU.add).then_inc(rs_in.sem, 1)
                dve.wait_ge(ln_gb_in.sem, ln_gb_in.at(layer, 32 * (s + 1)))
                for r in range(2):
                    xc = X[:, r, 0:512]
                    ins = stt(xc, xc, MV[:, r, 0:1], LNG[:, 0:512], ALU.subtract, ALU.mult)
                link(ins)
                link(newton(layer, 4 + s, 2))
                stt(NMR[:, :], MV[:, :, 0], -1.0, RR[:, 0:2], ALU.mult, ALU.mult).then_inc(rs_out.sem, 1)
                for r in range(2):
                    xc = X[:, r, 0:512]
                    ins = stt(xc, xc, RR[:, r:r + 1], LNB[:, 0:512], ALU.mult, ALU.add)
                ins.then_inc(x_ready.sem, 1)
                for ch in range(1, 4):
                    dve.wait_ge(ln_norm.sem, ln_norm.at(layer, 3 * s + ch))
                    xc = X[:, :, ch * 512:(ch + 1) * 512]
                    tt(xc, xc, bc(LNG[:, ch * 512:(ch + 1) * 512].unsqueeze(1), [P, 2, 512]), ALU.mult
                       ).then_inc(ln_mul.sem, 1)
                    if ch == 1 and then:
                        lo_split(layer, units[0], units[0])
                        then()
                        lo_split(layer, units[1], units[1])

            def gate_y(layer, p, k, half, passes, ready):
                dve.wait_ge(unit_done.sem, passes)
                dve.wait_ge(g_ready.sem, g_ready.at(layer, ready))
                for b in range(4):
                    if not (isinstance(k, int) and k + b < 2):
                        dve.wait_ge(x_add.sem, x_add.at(layer, k + b - 1))
                    col = half * UW + (b % 2) * 512
                    tt(R[:, b % 2, :], bank(p, b)[:, :], GB[:, col:col + 512], ALU.mult).then_inc(gated.sem, 1)

            def last_gate_y(layer, p, k, passes, ready):
                dve.wait_ge(unit_done.sem, passes)
                dve.wait_ge(g_ready.sem, g_ready.at(layer, ready))
                dve.wait_ge(x_add.sem, x_add.at(layer, k))
                for r in (1, 0):
                    for c in range(2):
                        col = UW + c * 512
                        tt(Y4[:, 2 * r + c, :], bank(p, 2 * r + c)[:, :], GB[:, col:col + 512], ALU.mult
                           ).then_inc(gated.sem, 1)
                for c in range(2):
                    xc = X[:, 0, UW + c * 512:UW + c * 512 + 512]
                    dve.wait_ge(gated.sem, gated.at(layer, k + c + 3))
                    tt(xc, xc, Y4[:, c, :], ALU.add).then_inc(x_add.sem, 2)

            def sub_layer_cols(layer, s):
                a0 = layer * 96 + 48 * s
                ts(SC[:, s, :], ADA[:, ds(a0 + 16, 16)], 1.0, None, ALU.add)
                dve.tensor_copy(SH[:, s, :], ADA[:, ds(a0, 16)]).then_inc(cols_set.sem, 1)

            def gate_cols(layer, k, a0, c0, n):
                g, hi = GC[:, c0:c0 + n], GCh[:, c0:c0 + n]
                link(ts(g, ADA[:, ds(layer * 96 + a0 + c0, n)], 1.0, None, ALU.add))
                link(dve.tensor_copy(hi, g))
                tt(GCl[:, c0:c0 + n], g, hi.bitcast(F32), ALU.subtract).then_inc(g_cols.sem, 1)

            def conv(layer, src, dst, j, t, last):
                dve.wait_ge(cv_in.sem, cv_in.at(layer, t + 1))
                for tap in (2, 1, 0):
                    sh = 3 - tap
                    ins = stt(dst[:, j, sh:SEQ], src[:, j, 0:SEQ - sh], cCW[:, tap, t:t + 1], dst[:, j, sh:SEQ],
                              ALU.mult, ALU.add)
                    if tap:
                        link(ins)
                if last:
                    ins.then_inc(cv_done.sem, 1)

            def hg_mask(layer, i, p):
                dve.wait_ge(hg_s.sem, hg_s.at(layer, i + 1))
                for b in range(2):
                    ins = tt(MS[:, 4 * b:4 * b + 4, :], work(p, 2 + b)[:, :].rearrange("p (l i) -> p l i", i=P),
                             LM[:, b * 512:(b + 1) * 512].rearrange("p (l i) -> p l i", i=P), ALU.mult)
                ins.then_inc(hg_ms.sem, 1)
                dve.wait_ge(hg_ms.sem, hg_ms.at(layer, i + 1))
                if i:
                    dve.wait_ge(hg_o.sem, hg_o.at(layer, i))
                dve.tensor_reduce(SM[:, :], MS[:, :, :].rearrange("p l i -> p i l"), AX.X, ALU.add
                                  ).then_inc(hg_sm.sem, 1)

            for n in range(W_SLOTS):
                lo_split(0, n, n)
            ada_out(4, 24, PB[4])
            with dve.Fori(0, DEPTH) as layer:
                link.start(layer)
                dve.wait_ge(ada_cols.sem, ada_cols.at(layer, 0))
                sub_layer_cols(layer, 0)
                dve.tensor_copy(cHGW[:, :], PT[:, ds(layer * 4 + T_HGW, 4)])
                dve.tensor_copy(cCB[:, :], PT[:, ds(layer * 12 + T_CB, 12)])
                dve.tensor_copy(cMNW[:, :], PT[:, ds(layer * 8 + T_MNW, 8)])
                dve.tensor_copy(cCW[:, :, :], PT[:, ds(layer * 48 + T_CW, 48)])
                dve.tensor_copy(cLB[:, :], LBT[:, ds(layer * 4, 4)])
                dve.tensor_copy(cOML[:, :], OML[:, ds(layer * 4, 4)])
                dve.tensor_copy(cMD[:, :], MD[:, ds(layer * 16, 16)])
                dve.tensor_copy(cDTB[:, :], DTB[:, ds(layer, 1)])
                dve.tensor_copy(cNA[:, :], NA[:, ds(layer, 1)])
                h_chunk(layer, 0, 0)
                for p in range(FF0):
                    for kt in range(KT):
                        n = p * KT + kt
                        at = (p, kt)
                        if n + AHEAD >= W_SLOTS and not by_pool(n + AHEAD):
                            lo_split(layer, n + AHEAD, n + AHEAD, width((n + AHEAD) // KT))
                        if p == 0 and kt in (3, 7, 11):
                            h_chunk(layer, 0, (kt + 1) // 4)
                        if n >= 2 and ada_due(n - 2, 24, 6) is not None:
                            half = ada_due(n - 2, 24, 6)
                            ada_out(ada_sum.at(layer, half + 1), layer * 96 + (4 + half) * 8,
                                    work(p, ada_bank(p)))
                        if at == (1, 3):
                            dve.wait_ge(set_free.sem, set_free.at(layer, 1))
                            for h in range(4):
                                fh = EQ[:, 2 * h:2 * h + 2, :]
                                ts(fh, fh, cOML[:, h:h + 1], cLB[:, h:h + 1], ALU.mult, ALU.add
                                   ).then_inc(hg_f.sem, 1)
                            dve.wait_ge(hg_f.sem, hg_f.at(layer, 4))
                            ts(KTt[:, :, :], EQ[:, :, :], -1.0, 1.0, ALU.mult, ALU.add).then_inc(hg_k.sem, 1)
                        if p in (2, 3) and kt in HG_X1:
                            i = (p - 2) * 4 + HG_X1.index(kt)
                            h, t = divmod(i, 2)
                            dve.wait_ge(hg_e.sem, hg_e.at(layer, i + 1))
                            if i >= 2:
                                dve.wait_ge(hg_s.sem, hg_s.at(layer, i - 1))
                            tt(EQ2[:, i % 2], E2[:, i % 2], bc(QT[:, h, t * P:(t + 1) * P].unsqueeze(1), [P, 8, P]),
                               ALU.mult).then_inc(hg_eq.sem, 1)
                        if p in (2, 3) and kt in HG_M:
                            hg_mask(layer, (p - 2) * 4 + HG_M.index(kt), p)
                        for a in ada_units(n, 24, 6):
                            ada_mul(ada_in[a % 2].sem, ada_in[0].at(layer, 16 * (a // 2 + 1)), ada_mac.at(layer, a),
                                    ada_sum.at(layer, a // 16), ADR[:, a % 2, :], a % 16)
                        if at in CONV:
                            j = CONV.index(at)
                            conv(layer, U, CV, j, j, j == 7)
                        if p == 4 and 3 <= kt <= 6:
                            conv(layer, BU, CB2, kt - 3, kt + 5, kt == 6)
                        if at == (4, 4):
                            dve.wait_ge(set_free.sem, set_free.at(layer, 4))
                            link(ts(DTW[0][:, :], DTR[:, :], cDTB[:, 0:1], None, ALU.add))
                            stt(DTW[1][:, :], DTW[0][:, :], -1.0, DTW[0][:, :], ALU.mult, ALU.max
                                ).then_inc(dt_abs.sem, 1)
                        if at == (4, 5):
                            dve.wait_ge(dt_exp.sem, dt_exp.at(layer, 1))
                            ts(DTW[2][:, :], DTW[1][:, :], 1.0, None, ALU.add).then_inc(dt_u.sem, 1)
                        if at == (4, 6):
                            dve.wait_ge(hg_oe.sem, hg_oe.at(layer, 8))
                            rms(layer, 1, 8, P)
                        if at == (4, 7):
                            dve.wait_ge(dt_ln.sem, dt_ln.at(layer, 1))
                            link(ts(DTW[2][:, :], DTW[2][:, :], -1.0, 1e-30, ALU.add, ALU.add))
                            link(dve.reciprocal(DTW[2][:, :], DTW[2][:, :]))
                            link(stt(DTW[3][:, :], DTW[3][:, :], 1e-30, DTW[2][:, :], ALU.add, ALU.mult))
                            link(tt(DTW[3][:, :], DTW[3][:, :], DTW[1][:, :], ALU.mult))
                            link(stt(DTT[:, :], DTW[0][:, :], 0.0, DTW[3][:, :], ALU.max, ALU.add))
                            link(ts(DTW[0][:, :], DTT[:, :], cNA[:, 0:1], None, ALU.mult))
                            dve.tensor_tensor_scan(CUM[:, :], bc(ones[0:16, :], [16, SEQ]), DTW[0][:, :], 0.0,
                                                   ALU.mult, ALU.add).then_inc(dt_cum.sem, 1)
                        if at == (4, 11):
                            t2_chunk(layer, 1, 4, 0, 4)
                        if at in ((4, 13), (4, 14)):
                            gr = kt - 13
                            dve.wait_ge(m_s.sem, m_s.at(layer, gr + 1))
                            tt(SB[:, gr, :], work(4, 3 if gr == 0 else 0)[:, 0:384], K[:, K_TRI:K_TRI + 384],
                               ALU.mult).then_inc(m_sm.sem, 1)
                        if p == 5 and kt in M_MUL:
                            i = M_MUL.index(kt)
                            dve.wait_ge(m_exp.sem, m_exp.at(layer, i + 1))
                            if i == 0:
                                dve.wait_ge(m_sm.sem, m_sm.at(layer, 2))
                            tt(MW[:, i % 2, :, :], MW[:, i % 2, :, :],
                               bc(SB[:, i // 4, :].unsqueeze(1), [P, 2, 384]), ALU.mult).then_inc(m_m.sem, 1)
                        if at in ((5, 10), (5, 15)):
                            gr = 0 if kt == 10 else 1
                            dve.wait_ge(m_y.sem, m_y.at(layer, 4 * gr + 4))
                            dve.wait_ge(xsd_ready.sem, xsd_ready.at(layer, 1))
                            for r in range(2):
                                xs = XS[:, r, gr * 512:(gr + 1) * 512]
                                ins = tt(xs, xs, work(5, r)[:, :], ALU.add)
                            ins.then_inc(m_ye.sem, 1)
                        if at == (6, 6):
                            for h in range(4):
                                dve.wait_ge(r_s.sem, r_s.at(layer, h // 2 + 1))
                                dg = K_DG + h * SEQ
                                tt(SR[:, h, 0:SEQ], work(6, h)[:, 0:SEQ], K[:, dg:dg + SEQ], ALU.mult)
                                tt(SR[:, h, SEQ:384], work(6, h)[:, SEQ:384], K[:, dg:dg + P], ALU.mult
                                   ).then_inc(r_sm.sem, 1)
                        if at == (6, 9):
                            dve.wait_ge(r_oe.sem, r_oe.at(layer, 1))
                            rms(layer, 2, 8, P)
                        if at == (6, 14):
                            t2_chunk(layer, 2, 0, 4, 4)
                        if at == (7, 2):
                            dve.wait_ge(set_free.sem, set_free.at(layer, 7))
                            dve.wait_ge(m_ye.sem, m_ye.at(layer, 2))
                            for r in range(2):
                                ins = tt(XS[:, r, :], XS[:, r, :], ZS[:, r, :], ALU.mult)
                            ins.then_inc(m_z.sem, 1)
                        if at == (7, 3):
                            dve.wait_ge(m_sq.sem, m_sq.at(layer, 1))
                            rms(layer, 3, 4, 512)
                            dve.wait_ge(rs_out.sem, rs_out.at(layer, 3))
                            for b in range(4):
                                xs = XS[:, b // 2, (b % 2) * 512:(b % 2 + 1) * 512]
                                ins = ts(xs, xs, RR[:, b:b + 1], None, ALU.mult)
                            ins.then_inc(m_rows.sem, 1)
                        if at == (7, 9):
                            t2_chunk(layer, 3, 8, 8, 8)
                        if at == (7, 11):
                            dve.wait_ge(ada_cols.sem, ada_cols.at(layer, 2))
                            gate_cols(layer, 1, 32, 0, 16)
                        if at == (8, 1):
                            gate_y(layer, 7, 0, 0, unit_done.at(layer, KT * (8)), 1)
                        if at == (8, 8):
                            row_stats(layer, (0, 1), x_add.at(layer, 4))
                dve.wait_ge(ada_cols.sem, ada_cols.at(layer, 6))
                sub_layer_cols(layer, 1)
                last_gate_y(layer, 8, 4, unit_done.at(layer, KT * FF0), 1)
                layer_norm_rows(layer, 0, row_stats(layer, (2, 3), x_add.at(layer, 8), 2),
                                [FF0 * KT + AHEAD, FF0 * KT + AHEAD + 1], lambda: h_chunk(layer, 1, 0))
                with dve.Fori(0, GROUPS) as g:
                    def group(ada):
                        for m in range(4 * KT):
                            s, kt = divmod(m, KT)
                            if W_SLOTS <= m + AHEAD < 4 * KT:
                                lo_split(layer, g * 64 + FF0 * KT + m + AHEAD, m + AHEAD)
                            if s == 0 and kt in (3, 7, 11):
                                with dve.If(g < 1):
                                    h_chunk(layer, 1, (kt + 1) // 4)
                            if ada and m >= 2 and ada_due(m - 2, 32, 2) is not None:
                                half = ada_due(m - 2, 32, 2)
                                ada_out(ada_sum.at(layer, g * 2 + 7 + half),
                                        ((layer * 12 + g * 2 + 10 + half) % 24) * 8, work(FF0 + s, 3))
                            for a in ada_units(m, 32, 2) if ada else ():
                                ada_mul(ada_in[a % 2].sem, ada_in[0].at(layer, g * 256 + 16 * (48 + a // 2 + 1)),
                                        ada_mac.at(layer, g * 32 + 96 + a), ada_sum.at(layer, g * 2 + 6 + a // 16),
                                        ADR[:, a % 2, :], a % 16)
                            if s in (1, 2) and kt == 1:
                                for b in range(4):
                                    k = g * 8 + 4 * (s - 1) + b
                                    dve.wait_ge(ff_hi.sem, ff_hi.at(layer, k + 1))
                                    t = 8 * (s - 1) + 2 * b
                                    tt(T2l[:, t:t + 2, :], SQ[:, b % 2, :].rearrange("p (a b) -> p a b", a=2),
                                       T2h[:, t:t + 2, :].bitcast(F32), ALU.subtract).then_inc(ff_ready.sem, 1)
                            if m == 1:
                                with dve.If(g > 0):
                                    gate_y(layer, FF0 + 3, g * 8 + 4, 1, unit_done.at(layer, KT * (g * 4 + FF0)), 3)
                            if ada and m in (34, 63):
                                with dve.If(g < 1):
                                    i = 0 if m == 34 else 1
                                    dve.wait_ge(ada_cols.sem, ada_cols.at(layer, 7 + i))
                                    gate_cols(layer, 2 + i, 80, 8 * i, 8)
                            if m == 49:
                                gate_y(layer, FF0 + 2, g * 8 + 8, 0, unit_done.at(layer, KT * (g * 4 + FF0 + 3)), 2)
                            if m == 58:
                                with dve.If(g > GROUPS - 2):
                                    row_stats(layer, (0, 1), x_add.at(layer, 36))

                    with dve.If(g + 2 * layer < 3):
                        group(True)
                    with dve.Else():
                        group(False)
                    with dve.If(g + GROUPS * layer < GROUPS * DEPTH - 1):
                        for m in range(4 * KT, 4 * KT + W_SLOTS):
                            lo_split(layer, g * 64 + FF0 * KT + m, m)
                last_gate_y(layer, FF0 + 3, 36, unit_done.at(layer, KT * NPASS), 3)
                layer_norm_rows(layer, 1, row_stats(layer, (2, 3), x_add.at(layer, 40), 4))
                link.end("dve")

        @block.tensor
        def _(pe):
            mm, tr = pe.matmul, pe.transpose

            def ada_sums(mac_count, bank_ap):
                pe.wait_ge(ada_mac.sem, mac_count)
                for i in range(8):
                    ins = mm(bank_ap[:, i:i + 1], ACC[:, i * P:(i + 1) * P], ones, start=True, stop=True)
                ins.then_inc(ada_sum.sem, 1)

            pe.wait_ge(pro_st.sem, 16 * 9)
            for j, rows in enumerate((P, P, 104)):
                ins = tr(PB[0][:, j * P:j * P + rows], ST[0:rows, j, :], ident[0:rows, 0:rows])
            ins.then_inc(pro_T.sem, 1)
            for q in range(4):
                if q:
                    pe.wait_ge(ada_cols.sem, q)
                else:
                    pe.wait_ge(pro_in.sem, 16 * 7)
                pe.wait_ge(ada_mac.sem, 16 * (q + 1) + 2)
                if q == 3:
                    pe.wait_ge(pro_dve.sem, 3)
                for i in range(8):
                    cols = slice(i * P, (i + 1) * P)
                    even, odd = PACC[q % 2]
                    ins = mm(PB[4][:, i:i + 1], even[:, cols], ones, start=True, stop=q == 3)
                    if q < 3:
                        ins = mm(PB[4][:, i:i + 1], odd[:, cols], ones, start=False, stop=True)
                ins.then_inc(ada_sum.sem, 1)
            pe.wait_ge(ada_cols.sem, 4)

            def x_transpose(layer, s, ch):
                pe.wait_ge(x_ready.sem, x_ready.at(layer, 4 * s + ch + 1) - 4)
                if ch >= 2:
                    pe.wait_ge(hT_hi.sem, hT_hi.at(layer, 16 * s + 4 * (ch - 1)))
                for b in (2 * ch, 2 * ch + 1):
                    for j in range(2):
                        for r in range(2):
                            kt = 2 * b + j
                            ins = tr(work(s * FF0, b % 4)[:, j * SEQ + r * P:j * SEQ + (r + 1) * P],
                                     X[:, r, kt * P:(kt + 1) * P], ident)
                    ins.then_inc(xT.sem, 1)

            def unit(layer, n, m, p, kt, left, kind, first, last):
                pe.wait_ge(*lo_ready(layer, n))
                k = m % W_SLOTS
                lh, ll = left
                if kind == "rows":
                    for r in range(2):
                        rows = slice(r * P, (r + 1) * P)
                        for i, (a, w) in enumerate(((lh, WH), (lh, WL), (ll, WH))):
                            for h in range(2):
                                ins = mm(bank(p, 2 * r + h)[:, :], a[:, kt, rows], w[:, k, h * 512:(h + 1) * 512],
                                         start=first and i == 0, stop=last and i == 2)
                else:
                    tiles = 4 if kind == "bc" else 8
                    for j in range(tiles):
                        dst = bank(p, j // 2)[:, (j % 2) * SEQ:(j % 2 + 1) * SEQ]
                        cols = slice(j * P, (j + 1) * P)
                        for i, (a, w) in enumerate(((lh, WH), (ll, WH), (lh, WL))):
                            ins = mm(dst, w[:, k, cols], a[:, kt, :], start=first and i == 0 and j % 2 == 0,
                                     stop=last and i == 2, skip_group_check=True)
                    if kind == "bc":
                        for i, (a, w) in enumerate(((lh, WH), (ll, WH), (lh, WL))):
                            ins = mm(bank(p, 2)[:, 0:SEQ], w[:, k, 512:640], a[:, kt, :],
                                     start=first and i == 0, stop=last and i == 2)
                ins.then_inc(unit_done.sem, 1)

            def hg_levels(layer, i, p):
                h, t = divmod(i, 2)
                f = LF[:, t, h * P:(h + 1) * P]
                if i % 4:
                    pe.wait_ge(hg_e.sem, hg_e.at(layer, i))
                if i - 2 in HG_EARLY:
                    pe.wait_ge(hg_sx.sem, hg_sx.at(layer, (i - 1) // 2))
                mm(work(p, 0)[:, :], f, K[:, K_ML:K_ML + 512], start=True, stop=True)
                last = K_ML + (7 + t) * P
                mm(work(p, 1)[:, 0:384], f, K[:, K_ML + 512:K_ML + 896], start=True, stop=True)
                mm(work(p, 1)[:, 384:512], f, K[:, last:last + P], start=True, stop=True).then_inc(hg_x.sem, 1)

            def hg_scores(layer, i, p):
                h, t = divmod(i, 2)
                rows = slice(t * P, (t + 1) * P)
                pe.wait_ge(hg_ek.sem, hg_ek.at(layer, i + 1))
                if i and HG_O[i - 1][0] == p:
                    pe.wait_ge(hg_oe.sem, hg_oe.at(layer, i))
                for lv in range(7):
                    mm(work(p, 2 + lv // 4)[:, (lv % 4) * P:(lv % 4 + 1) * P], E2[:, i % 2, lv, :], EQ2[:, i % 2, lv, :],
                       start=True, stop=True)
                if t == 1:
                    if i in HG_EARLY:
                        pe.wait_ge(hg_e.sem, hg_e.at(layer, i + 2))
                    mm(work(p, 0)[:, 0:P], CROSSK[:, :], EQ2[:, i % 2, 7, :], start=True, stop=True)
                mm(work(p, 3)[:, 384:512], KTt[:, h, rows], QT[:, h, rows], start=True, stop=True
                   ).then_inc(hg_s.sem, 1)

            def hg_output(layer, i, p):
                h, t = divmod(i, 2)
                cols = slice(h * P, (h + 1) * P)
                pe.wait_ge(hg_sm.sem, hg_sm.at(layer, i + 1))
                o = work(p, 2)[:, 0:P]
                ins = mm(o, SM[:, :], V[:, t, cols], start=True, stop=(t == 0))
                if t == 1:
                    pe.wait_ge(hg_sx.sem, hg_sx.at(layer, (i + 1) // 2))
                    ins = mm(o, SX[:, :], V[:, 0, cols], start=False, stop=True)
                ins.then_inc(hg_o.sem, 1)

            def rows_to_t2(src, bank_of, n):
                for j in range(n):
                    for r in range(2):
                        ins = tr(bank_of(j // 2)[:, (j % 2) * SEQ + r * P:(j % 2) * SEQ + (r + 1) * P],
                                 src[:, r, j * P:(j + 1) * P], ident)
                ins.then_inc(t2_T.sem, 1)

            def gate_broadcast(layer, k, p, kts):
                pe.wait_ge(g_cols.sem, g_cols.at(layer, k))
                for i, kt in enumerate(kts):
                    dst = work(p, i // 4)[:, (i % 4) * P:(i % 4 + 1) * P]
                    mm(dst, bc(GCh[:, kt:kt + 1], [P, P]), IDR[:, :], start=True, stop=False)
                    ins = mm(dst, bc(GCl[:, kt:kt + 1], [P, P]), IDR[:, :], start=False, stop=True)
                ins.then_inc(g_bc.sem, 1)

            with pe.Fori(0, DEPTH) as layer:
                for p in range(FF0):
                    kind = "bc" if p == 3 else "cols" if p in (0, 2) else "rows"
                    if p == 1:
                        pe.wait_ge(hT_hi.sem, hT_hi.at(layer, 16))
                    if p >= 2:
                        pe.wait_ge(set_free.sem, set_free.at(layer, p - 1))
                    if p == 3:
                        pe.wait_ge(hg_ms.sem, hg_ms.at(layer, 4))
                        pe.wait_ge(hg_sx.sem, hg_sx.at(layer, 2))
                    if p == 4:
                        pe.wait_ge(hg_ms.sem, hg_ms.at(layer, 8))
                        pe.wait_ge(hg_sx.sem, hg_sx.at(layer, 4))
                    if p == 5:
                        pe.wait_ge(m_sm.sem, m_sm.at(layer, 2))
                        pe.wait_ge(dt_ready.sem, dt_ready.at(layer, 1))
                    if p == 6:
                        pe.wait_ge(m_ye.sem, m_ye.at(layer, 2))
                        pe.wait_ge(ada_cols.sem, ada_cols.at(layer, 4))
                    if p == 7:
                        pe.wait_ge(t2_hi.sem, t2_hi.at(layer, 8))
                    if p == 8:
                        pe.wait_ge(g_ready.sem, g_ready.at(layer, 1))
                    for kt in range(KT):
                        n = p * KT + kt
                        at = (p, kt)
                        if n >= 3 and ada_due(n - 3, 24, 6) is not None:
                            pe.wait_ge(ada_cols.sem, ada_cols.at(layer, ada_due(n - 3, 24, 6) + 1))
                        if p == 0 and kt in (0, 2, 6, 10):
                            x_transpose(layer, 0, (kt + 2) // 4)
                        if p == 0:
                            pe.wait_ge(hT_ready.sem, hT_ready.at(layer, kt + 1))
                        if at == (1, 8):
                            pe.wait_ge(hg_lnf.sem, hg_lnf.at(layer, 1))
                            for h in range(4):
                                for t in range(2):
                                    ins = tr(work(1, t)[:, h * P:(h + 1) * P], E[:, 2 * h + t, :], ident)
                            ins.then_inc(hg_logT.sem, 1)
                        if p in (2, 3) and kt in HG_X:
                            i = (p - 2) * 4 + HG_X.index(kt)
                            if i == 0:
                                pe.wait_ge(hg_log.sem, hg_log.at(layer, 1))
                            if i in (0, 4):
                                pe.wait_ge(set_free.sem, set_free.at(layer, p))
                            hg_levels(layer, i, p)
                        if p in (2, 3) and kt in HG_S:
                            hg_scores(layer, (p - 2) * 4 + HG_S.index(kt), p)
                        if at in HG_O:
                            if at == (4, 4):
                                pe.wait_ge(set_free.sem, set_free.at(layer, 4))
                            hg_output(layer, HG_O.index(at), p)
                        if at == (4, 8):
                            pe.wait_ge(cv_act.sem, cv_act.at(layer, 1))
                            pe.wait_ge(hg_oe.sem, hg_oe.at(layer, 8))
                            for r in range(2):
                                for j in range(8):
                                    ins = tr(work(4, 2 * r + j // 4)[:, (j % 4) * P:(j % 4 + 1) * P],
                                             U[:, j, r * P:(r + 1) * P], ident)
                                ins.then_inc(xs_T.sem, 1)
                        if at == (4, 10):
                            pe.wait_ge(xs_rows.sem, xs_rows.at(layer, 1))
                            pe.wait_ge(hg_rows.sem, hg_rows.at(layer, 1))
                            rows_to_t2(LF, lambda b: work(4, b), 4)
                        if at == (4, 11):
                            pe.wait_ge(xs_rows.sem, xs_rows.at(layer, 2))
                            pe.wait_ge(dt_cum.sem, dt_cum.at(layer, 1))
                            for r in range(2):
                                for w, src in enumerate((DTT, CUM)):
                                    c0 = (2 * r + w) * 16
                                    ins = mm(work(4, 2)[:, c0:c0 + 16], src[:, r * P:(r + 1) * P],
                                             ident[0:16, 0:16], start=True, stop=True)
                            ins.then_inc(dt_rows.sem, 1)
                        if at in ((4, 12), (4, 13)):
                            gr = kt - 12
                            if gr == 0:
                                pe.wait_ge(cv_act.sem, cv_act.at(layer, 2))
                            else:
                                pe.wait_ge(t2_hi.sem, t2_hi.at(layer, 4))
                            b_ = work(4, 3 if gr == 0 else 0)
                            mm(b_[:, 0:SEQ], BC[:, gr, 0:P], BC[:, 2 + gr, :], start=True, stop=True)
                            mm(b_[:, SEQ:384], BC[:, gr, P:SEQ], BC[:, 2 + gr, P:SEQ], start=True, stop=True
                               ).then_inc(m_s.sem, 1)
                        if p == 5 and kt in M_CUM:
                            i = M_CUM.index(kt)
                            if i == 0:
                                pe.wait_ge(set_free.sem, set_free.at(layer, 5))
                            if i >= 2:
                                pe.wait_ge(m_arg.sem, m_arg.at(layer, i - 1))
                            for e in range(2):
                                hd = 2 * i + e
                                ins = mm(work(5, 2 + i % 2)[:, e * SEQ:(e + 1) * SEQ],
                                         bc(ident[0:16, hd:hd + 1], [16, P]), CUM[:, :], start=True, stop=True)
                            ins.then_inc(m_cum.sem, 1)
                        if p == 5 and kt in M_Y:
                            i = M_Y.index(kt)
                            pe.wait_ge(m_m.sem, m_m.at(layer, i + 1))
                            if i == 0:
                                pe.wait_ge(xd_ready.sem, xd_ready.at(layer, 1))
                            if i == 4:
                                pe.wait_ge(m_ye.sem, m_ye.at(layer, 1))
                            for e in range(2):
                                hd = 2 * i + e
                                v = slice(hd * 64, (hd + 1) * 64)
                                y = slice((hd % 8) * 64, (hd % 8 + 1) * 64)
                                mm(work(5, 0)[:, y], MW[:, i % 2, e, 0:P], XD[:, 0, v], start=True, stop=True)
                                mm(work(5, 1)[:, y], MW[:, i % 2, e, P:SEQ], XD[:, 0, v], start=True, stop=False)
                                ins = mm(work(5, 1)[:, y], MW[:, i % 2, e, SEQ:384], XD[:, 1, v], start=False,
                                         stop=True)
                            ins.then_inc(m_y.sem, 1)
                        if at == (6, 3):
                            pe.wait_ge(set_free.sem, set_free.at(layer, 6))
                            pe.wait_ge(r_rot.sem, r_rot.at(layer, 1))
                            for w in range(2):
                                for h in range(4):
                                    for t in range(2):
                                        c0 = w * 512 + h * P
                                        ins = tr(work(6, 2 * w + h // 2)[:, (h % 2) * SEQ + t * P:
                                                                         (h % 2) * SEQ + (t + 1) * P],
                                                 QK[:, t, c0:c0 + P], ident)
                            ins.then_inc(r_T.sem, 1)
                        if at == (6, 5):
                            pe.wait_ge(r_Te.sem, r_Te.at(layer, 1))
                            for h in range(4):
                                mm(work(6, h)[:, 0:SEQ], RKT[:, h, 0:P], RQT[:, h, :], start=True, stop=True)
                                ins = mm(work(6, h)[:, SEQ:384], RKT[:, h, P:SEQ], RQT[:, h, P:SEQ], start=True,
                                         stop=True)
                                if h % 2:
                                    ins.then_inc(r_s.sem, 1)
                        if at == (6, 8):
                            pe.wait_ge(r_sm.sem, r_sm.at(layer, 4))
                            for h in range(4):
                                c = slice(h * P, (h + 1) * P)
                                mm(work(6, 0)[:, c], SR[:, h, 0:P], RVv[:, 0, c], start=True, stop=True)
                                mm(work(6, 1)[:, c], SR[:, h, P:SEQ], RVv[:, 0, c], start=True, stop=False)
                                ins = mm(work(6, 1)[:, c], SR[:, h, SEQ:384], RVv[:, 1, c], start=False, stop=True)
                            ins.then_inc(r_o.sem, 1)
                        if at == (6, 13):
                            pe.wait_ge(r_rows.sem, r_rows.at(layer, 1))
                            rows_to_t2(RO, lambda b: work(6, 2 + b), 4)
                        if at == (7, 8):
                            pe.wait_ge(set_free.sem, set_free.at(layer, 7))
                            pe.wait_ge(m_rows.sem, m_rows.at(layer, 1))
                            rows_to_t2(XS, lambda b: work(7, b), 8)
                        if at == (7, 12):
                            gate_broadcast(layer, 1, 7, range(16))
                        if p >= 7:
                            pe.wait_ge(t2_ready.sem, t2_ready.at(layer, kt + 1 if p == 7 else 16))
                            left, lk = (T2h, T2l), OUT_ORDER[kt]
                        else:
                            left, lk = (HTh, HTl), kt
                        unit(layer, n, n, p, lk, left, kind, kt == 0, kt == KT - 1)
                        if ada_due(n, 24, 6) is not None:
                            half = ada_due(n, 24, 6)
                            b_ = ada_bank(p)
                            if p == 1:
                                pe.wait_ge(set_free.sem, set_free.at(layer, 1))
                            if p == 2:
                                pe.wait_ge(hg_e.sem, hg_e.at(layer, 4))
                            if p == 5:
                                pe.wait_ge(m_arg.sem, m_arg.at(layer, 8))
                            if p == 7:
                                pe.wait_ge(set_free.sem, set_free.at(layer, 7))
                            if p == 8:
                                pe.wait_ge(gated.sem, gated.at(layer, 4))
                            ada_sums(ada_mac.at(layer, 16 * (half + 1)), work(p, b_))
                with pe.Fori(0, GROUPS) as g:
                    for m in range(4 * KT):
                        s, kt = divmod(m, KT)
                        p = FF0 + s
                        if kt == 0:
                            if s == 0:
                                pe.wait_ge(ada_cols.sem, ada_cols.at(layer, 6))
                            if s < 2:
                                pe.wait_ge(gated.sem, gated.at(layer, g * 8 + 4 + 4 * s))
                            else:
                                pe.wait_ge(ff_relu.sem, ff_relu.at(layer, g * 8 + 4 * (s - 1)))
                            if s == 1:
                                pe.wait_ge(hT_hi.sem, hT_hi.at(layer, 32))
                        if s == 0 and kt in (0, 2, 6, 10):
                            with pe.If(g < 1):
                                x_transpose(layer, 1, (kt + 2) // 4)
                        if s == 0:
                            pe.wait_ge(hT_ready.sem, hT_ready.at(layer, 16 + kt + 1))
                        if s == 2 and kt % 2 == 0:
                            pe.wait_ge(ff_ready.sem, ff_ready.at(layer, g * 8 + kt // 2 + 1))
                        if m == 35:
                            with pe.If(g < 1):
                                pe.wait_ge(ff_relu.sem, ff_relu.at(layer, 8))
                                gate_broadcast(layer, 2, p, range(8))
                        left = (HTh, HTl) if s < 2 else (T2h, T2l)
                        unit(layer, g * 64 + FF0 * KT + m, m, p, kt, left, "cols" if s < 2 else "rows",
                             kt == 0, kt == KT - 1)
                        if ada_due(m, 32, 2) is not None:
                            half = ada_due(m, 32, 2)
                            with pe.If(g + 2 * layer < 3):
                                if s == 1:
                                    pe.wait_ge(ff_relu.sem, ff_relu.at(layer, g * 8 + 4))
                                else:
                                    pe.wait_ge(gated.sem, gated.at(layer, g * 8 + 12))
                                ada_sums(ada_mac.at(layer, g * 32 + 96 + 16 * (half + 1)), work(p, 3))
                        if m >= 3 and ada_due(m - 3, 32, 2) is not None:
                            with pe.If(g + 2 * layer < 3):
                                pe.wait_ge(ada_cols.sem, ada_cols.at(layer, g * 2 + 7 + ada_due(m - 3, 32, 2)))
                        if m == 63:
                            with pe.If(g < 1):
                                gate_broadcast(layer, 3, p, range(8, 16))
                                pe.wait_ge(g_ready.sem, g_ready.at(layer, 3))


_INS = ["x", "c", "positions", "lb_logits", "w_in", "w_out", "w_ada", "b_ada", "ln_g", "ln_b", "hg_norm_w",
        "m_conv_w", "m_conv_b", "m_dt_bias", "m_a_log", "m_d", "m_norm_w", "w1", "w2"]


def kernel(**inputs):
    import concourse.bacc as _bacc
    from concourse.bass_utils import run_bass_kernel_spmd as _run

    nc = _bacc.Bacc("TRN2", target_bir_lowering=False, num_devices=1)
    nc.disable_value_cache = True
    arrays, args = {}, []
    for name in _INS + ["consts"]:
        a = constants() if name == "consts" else np.ascontiguousarray(inputs[name])
        arrays[f"in_{name}"] = a
        args.append(nc.dram_tensor(f"in_{name}", a.shape, mybir.dt.from_np(a.dtype), kind="ExternalInput").ap())
    args.append(nc.dram_tensor("out_0", (1, SEQ, D), F32, kind="ExternalOutput").ap())
    hybrid_trunk(nc, *args)
    r = _run(nc, [arrays], core_ids=[0])
    return r.results[0]["out_0"]
```
